# Optimizing a Trainium2 kernel written in Bass

```python
import math
import jax, jax.numpy as jnp
from jax import lax
import numpy as np

D_MODEL = 1024
BATCH = 1
SEQ = 256
DEPTH = 1

HEAD_DIM = 64
N_HEADS_TOTAL = D_MODEL // HEAD_DIM
N_HEADS_MOBA = N_HEADS_TOTAL // 2
N_HEADS_SWA = N_HEADS_TOTAL - N_HEADS_MOBA
N_KV_SWA = 2
GQA_GROUP = N_HEADS_SWA // N_KV_SWA
MIX_WIDTH = N_HEADS_TOTAL * HEAD_DIM
MOBA_BLOCK = 256
MOBA_TOPK = 3
MOBA_QCHUNK = 16
SWA_WINDOW = 128
N_BUCKETS = 32
MAX_DISTANCE = 128
D_FF = 4 * D_MODEL
EPS = 1e-6
W_A = N_HEADS_MOBA * HEAD_DIM
W_QB = N_HEADS_SWA * HEAD_DIM
W_KVB = N_KV_SWA * HEAD_DIM
D_IN = 3 * W_A + W_QB + 2 * W_KVB


def rmsnorm(x, g):
    xf = x.astype(jnp.float32)
    y = xf * lax.rsqrt(jnp.mean(xf * xf, axis=-1, keepdims=True) + EPS)
    return (y * g.astype(jnp.float32)).astype(x.dtype)

def t5_bucket(dist):
    n = jnp.maximum(dist, 0)
    max_exact = N_BUCKETS // 2
    nf = jnp.maximum(n, 1).astype(jnp.float32)
    large = max_exact + (jnp.log(nf / max_exact) / math.log(MAX_DISTANCE / max_exact)
                         * (N_BUCKETS - max_exact)).astype(jnp.int32)
    large = jnp.minimum(large, N_BUCKETS - 1)
    return jnp.where(n < max_exact, n, large)

def moba_attention(q, k, v, bias_hb):
    B, H, S, dh = q.shape
    nb = -(-S // MOBA_BLOCK)
    sp = nb * MOBA_BLOCK
    padw = ((0, 0), (0, 0), (0, sp - S), (0, 0))
    q, k, v = jnp.pad(q, padw), jnp.pad(k, padw), jnp.pad(v, padw)
    kb = k.reshape(B, H, nb, MOBA_BLOCK, dh)
    vb = v.reshape(B, H, nb, MOBA_BLOCK, dh)
    k_mean = jnp.mean(kb.astype(jnp.float32), axis=3)
    gate = jnp.einsum('bhsd,bhnd->bhsn', q.astype(jnp.float32), k_mean)
    q_block = jnp.arange(sp) // MOBA_BLOCK
    fully_past = jnp.arange(nb)[None, :] < q_block[:, None]
    gate = jnp.where(fully_past, gate, -jnp.inf)
    n_sel = min(MOBA_TOPK, nb)
    sel_score, sel_idx = lax.top_k(gate, n_sel)
    sel_valid = jnp.isfinite(sel_score)
    scale = dh ** -0.5
    b_idx = jnp.arange(B)[:, None, None, None]
    h_idx = jnp.arange(H)[None, :, None, None]
    offs = jnp.arange(MOBA_BLOCK)

    def chunk(ci):
        q0 = ci * MOBA_QCHUNK
        qc = lax.dynamic_slice_in_dim(q, q0, MOBA_QCHUNK, axis=2)
        idx = lax.dynamic_slice_in_dim(sel_idx, q0, MOBA_QCHUNK, axis=2)
        valid = lax.dynamic_slice_in_dim(sel_valid, q0, MOBA_QCHUNK, axis=2)
        qpos = q0 + jnp.arange(MOBA_QCHUNK)
        k_sel = kb[b_idx, h_idx, idx]
        v_sel = vb[b_idx, h_idx, idx]
        s_sel = jnp.einsum('bhqd,bhqnjd->bhqnj', qc, k_sel).astype(jnp.float32) * scale
        kpos_sel = idx[..., None] * MOBA_BLOCK + offs
        s_sel = s_sel + bias_hb[h_idx[..., None], t5_bucket(qpos[:, None, None] - kpos_sel)]
        s_sel = jnp.where(valid[..., None], s_sel, -jnp.inf)
        ob = q0 // MOBA_BLOCK
        k_own = lax.dynamic_slice_in_dim(k, ob * MOBA_BLOCK, MOBA_BLOCK, axis=2)
        v_own = lax.dynamic_slice_in_dim(v, ob * MOBA_BLOCK, MOBA_BLOCK, axis=2)
        s_own = jnp.einsum('bhqd,bhjd->bhqj', qc, k_own).astype(jnp.float32) * scale
        dist = qpos[:, None] - (ob * MOBA_BLOCK + offs)[None, :]
        s_own = s_own + bias_hb[:, t5_bucket(dist)][None]
        s_own = jnp.where(dist >= 0, s_own, -jnp.inf)
        logits = jnp.concatenate(
            [s_sel.reshape(B, H, MOBA_QCHUNK, n_sel * MOBA_BLOCK), s_own], axis=-1)
        p = jax.nn.softmax(logits, axis=-1)
        p_sel = p[..., :n_sel * MOBA_BLOCK].reshape(B, H, MOBA_QCHUNK, n_sel, MOBA_BLOCK).astype(v.dtype)
        p_own = p[..., n_sel * MOBA_BLOCK:].astype(v.dtype)
        return (jnp.einsum('bhqnj,bhqnjd->bhqd', p_sel, v_sel)
                + jnp.einsum('bhqj,bhjd->bhqd', p_own, v_own))

    outs = lax.map(chunk, jnp.arange(sp // MOBA_QCHUNK))
    out = jnp.moveaxis(outs, 0, 2).reshape(B, H, sp, dh)
    return out[:, :, :S]

def swa_attention(q, k, v, bias_hb, sinks):
    B, HKV, G, S, dh = q.shape
    W = SWA_WINDOW
    nbq = S // W
    qb = q.reshape(B, HKV, G, nbq, W, dh)
    kb = k.reshape(B, HKV, nbq, W, dh)
    vb = v.reshape(B, HKV, nbq, W, dh)
    pad_prev = ((0, 0), (0, 0), (1, 0), (0, 0), (0, 0))
    k_band = jnp.concatenate([jnp.pad(kb[:, :, :-1], pad_prev), kb], axis=3)
    v_band = jnp.concatenate([jnp.pad(vb[:, :, :-1], pad_prev), vb], axis=3)
    s = jnp.einsum('bkgnqd,bknjd->bkgnqj', qb, k_band).astype(jnp.float32) * (dh ** -0.5)
    blk = jnp.arange(nbq)
    qpos = blk[:, None] * W + jnp.arange(W)[None, :]
    kpos = (blk[:, None] - 1) * W + jnp.arange(2 * W)[None, :]
    dist = qpos[:, :, None] - kpos[:, None, :]
    allowed = (dist >= 0) & (dist < W) & (kpos[:, None, :] >= 0)
    bias = bias_hb[:, t5_bucket(dist)].reshape(HKV, G, nbq, W, 2 * W)
    s = jnp.where(allowed, s + bias, -jnp.inf)
    sink = jnp.broadcast_to(sinks.astype(jnp.float32).reshape(1, HKV, G, 1, 1, 1), s.shape[:-1] + (1,))
    p = jax.nn.softmax(jnp.concatenate([s, sink], axis=-1), axis=-1)[..., :-1]
    out = jnp.einsum('bkgnqj,bknjd->bkgnqd', p.astype(v.dtype), v_band)
    return out.reshape(B, HKV, G, S, dh)

def token_mixer(h, w_in, w_out, sinks, bias_hb):
    B, S, _ = h.shape
    proj = h @ w_in
    qa, ka, va, qb, kb, vb = jnp.split(
        proj, [W_A, 2 * W_A, 3 * W_A, 3 * W_A + W_QB, 3 * W_A + W_QB + W_KVB], axis=-1)
    heads = lambda t, n: t.reshape(B, S, n, HEAD_DIM).transpose(0, 2, 1, 3)
    out_a = moba_attention(heads(qa, N_HEADS_MOBA), heads(ka, N_HEADS_MOBA),
                           heads(va, N_HEADS_MOBA), bias_hb[:N_HEADS_MOBA])
    out_a = out_a.transpose(0, 2, 1, 3).reshape(B, S, W_A)
    q_swa = qb.reshape(B, S, N_KV_SWA, GQA_GROUP, HEAD_DIM).transpose(0, 2, 3, 1, 4)
    out_b = swa_attention(q_swa, heads(kb, N_KV_SWA), heads(vb, N_KV_SWA),
                          bias_hb[N_HEADS_MOBA:], sinks)
    out_b = out_b.transpose(0, 3, 1, 2, 4).reshape(B, S, W_QB)
    return jnp.concatenate([out_a, out_b], axis=-1) @ w_out

def first_inputs(seed: int = 0) -> dict:
    key = jax.random.key(seed)
    ks = jax.random.split(key, 13)
    f32 = jnp.float32
    nrm = lambda k, shape, s: jax.random.normal(k, shape, f32) * s
    return {
        "x": nrm(ks[0], (BATCH, SEQ, D_MODEL), 1.0),
        "c": nrm(ks[1], (BATCH, D_MODEL), 1.0),
        "w_in": nrm(ks[2], (DEPTH, D_MODEL, D_IN), D_MODEL ** -0.5),
        "w_out": nrm(ks[3], (DEPTH, MIX_WIDTH, D_MODEL), MIX_WIDTH ** -0.5),
        "sinks": nrm(ks[4], (DEPTH, N_HEADS_SWA), 0.5),
        "rel_bias": nrm(ks[5], (N_BUCKETS, N_HEADS_TOTAL), 0.5),
        "w_ada": nrm(ks[6], (DEPTH, D_MODEL, 6 * D_MODEL), D_MODEL ** -0.5),
        "b_ada": nrm(ks[7], (DEPTH, 6 * D_MODEL), 0.02),
        "norm_gains": 1.0 + nrm(ks[8], (DEPTH, 4, D_MODEL), 0.05),
        "w1": nrm(ks[9], (DEPTH, D_MODEL, D_FF), D_MODEL ** -0.5),
        "b1": nrm(ks[10], (DEPTH, D_FF), 0.02),
        "w2": nrm(ks[11], (DEPTH, D_FF, D_MODEL), D_FF ** -0.5),
        "b2": nrm(ks[12], (DEPTH, D_MODEL), 0.02),
    }

def first_block(x, c, w_in, w_out, sinks, rel_bias, w_ada, b_ada, norm_gains, w1, b1, w2, b2):
    bias_hb = rel_bias.T
    c_act = jax.nn.silu(c)
    for l in range(DEPTH):
        mod = c_act @ w_ada[l] + b_ada[l]
        sh1, sc1, g1, sh2, sc2, g2 = [m[:, None, :] for m in jnp.split(mod, 6, axis=-1)]
        h = rmsnorm(x, norm_gains[l, 0]) * (1.0 + sc1) + sh1
        y = token_mixer(h, w_in[l], w_out[l], sinks[l], bias_hb)
        x = x + g1 * rmsnorm(y, norm_gains[l, 1])
        h = rmsnorm(x, norm_gains[l, 2]) * (1.0 + sc2) + sh2
        y = jnp.square(jax.nn.relu(h @ w1[l] + b1[l])) @ w2[l] + b2[l]
        x = x + g2 * rmsnorm(y, norm_gains[l, 3])
    return x


MLSTM_HEADS = 4
MLSTM_DH = 128
MLSTM_W = MLSTM_HEADS * MLSTM_DH
MLSTM_CHUNK = 128
CONV_W = 5
N_MGATES = 4 * MLSTM_HEADS

DIFF_HEADS = 4
DIFF_DH = 64
DIFF_DV = 2 * DIFF_DH
DIFF_QK_W = DIFF_HEADS * 2 * DIFF_DH
DIFF_W = DIFF_HEADS * DIFF_DV
Q_BLOCK = 128

OFF_MQ = 0
OFF_MK = OFF_MQ + MLSTM_W
OFF_MV = OFF_MK + MLSTM_W
OFF_MO = OFF_MV + MLSTM_W
OFF_MG = OFF_MO + MLSTM_W
OFF_DQ = OFF_MG + N_MGATES
OFF_DK = OFF_DQ + DIFF_QK_W
OFF_DV = OFF_DK + DIFF_QK_W
OFF_GATE = OFF_DV + DIFF_W
N_BRANCH = 2
IN_COLS = OFF_GATE + N_BRANCH * D_MODEL

N_EXPERTS = 16
EC_CAPACITY = 2
D_FF_EXPERT = 2 * D_MODEL


def rms_norm(x, g):
    xf = x.astype(jnp.float32)
    xf = xf * lax.rsqrt(jnp.mean(xf * xf, axis=-1, keepdims=True) + EPS)
    return (xf * g.astype(jnp.float32)).astype(x.dtype)

def centred_dwconv(x, w, b):
    c = x.shape[-1]
    pad = CONV_W // 2
    y = lax.conv_general_dilated(x, w[:, None, :].astype(x.dtype), window_strides=(1,),
                                 padding=[(pad, pad)], dimension_numbers=('NWC', 'WIO', 'NWC'),
                                 feature_group_count=c)
    return y + b.astype(x.dtype)

def mlstm_chunkwise(q, k, v, i_pre, f_pre):
    B, H, S, dk = q.shape
    dv = v.shape[-1]
    L = MLSTM_CHUNK
    NC = S // L
    q = q.astype(jnp.float32).reshape(B, H, NC, L, dk)
    k = (k.astype(jnp.float32) * dk ** -0.5).reshape(B, H, NC, L, dk)
    v = v.astype(jnp.float32).reshape(B, H, NC, L, dv)
    log_f = jax.nn.log_sigmoid(f_pre).reshape(B, H, NC, L)
    log_i = i_pre.reshape(B, H, NC, L)
    b = jnp.cumsum(log_f, axis=-1)
    g = b[..., -1]
    a = g[..., None] - b + log_i
    a_max = a.max(-1)
    w = jnp.exp(a - a_max[..., None])
    C_loc = jnp.einsum('bhclv,bhclk->bhcvk', v * w[..., None], k)
    n_loc = jnp.einsum('bhcl,bhclk->bhck', w, k)

    def step(carry, inp):
        C, n, m = carry
        C_l, n_l, am, gc = inp
        m_new = jnp.maximum(gc + m, am)
        sp = jnp.exp(gc + m - m_new)
        sl = jnp.exp(am - m_new)
        C_new = sp[..., None, None] * C + sl[..., None, None] * C_l
        n_new = sp[..., None] * n + sl[..., None] * n_l
        return (C_new, n_new, m_new), (C, n, m)

    xs = (jnp.moveaxis(C_loc, 2, 0), jnp.moveaxis(n_loc, 2, 0),
          jnp.moveaxis(a_max, 2, 0), jnp.moveaxis(g, 2, 0))
    init = (jnp.zeros((B, H, dv, dk), jnp.float32), jnp.zeros((B, H, dk), jnp.float32),
            jnp.zeros((B, H), jnp.float32))
    _, (C_in, n_in, m_in) = lax.scan(step, init, xs)
    C_in = jnp.moveaxis(C_in, 0, 2)
    n_in = jnp.moveaxis(n_in, 0, 2)
    m_in = jnp.moveaxis(m_in, 0, 2)

    lower = jnp.tril(jnp.ones((L, L), dtype=bool))
    D = b[..., :, None] - b[..., None, :] + log_i[..., None, :]
    D = jnp.where(lower, D, -jnp.inf)
    inter = b + m_in[..., None]
    m_t = jnp.maximum(inter, D.max(-1))
    P = jnp.exp(D - m_t[..., None])
    W = jnp.einsum('bhctd,bhcsd->bhcts', q, k) * P
    s_in = jnp.exp(inter - m_t)
    num = (jnp.einsum('bhcts,bhcsv->bhctv', W, v)
           + s_in[..., None] * jnp.einsum('bhcvk,bhctk->bhctv', C_in, q))
    den = W.sum(-1) + s_in * jnp.einsum('bhck,bhctk->bhct', n_in, q)
    h = num / jnp.maximum(jnp.abs(den), jnp.exp(-m_t))[..., None]
    return h.reshape(B, H, S, dv)

def mlstm_branch(z, conv_w, conv_b, b_mgate, norm_g):
    B, S, _ = z.shape
    qk = jax.nn.silu(centred_dwconv(z[..., OFF_MQ:OFF_MV], conv_w, conv_b))
    to_heads = lambda t: t.reshape(B, S, MLSTM_HEADS, MLSTM_DH).transpose(0, 2, 1, 3)
    q = to_heads(qk[..., :MLSTM_W])
    k = to_heads(qk[..., MLSTM_W:])
    v = to_heads(z[..., OFF_MV:OFF_MO])
    o = z[..., OFF_MO:OFF_MG]
    gates = z[..., OFF_MG:OFF_MG + N_MGATES].astype(jnp.float32) + b_mgate.astype(jnp.float32)
    gates = gates.reshape(B, S, 2, 2, MLSTM_HEADS).transpose(2, 3, 0, 4, 1)
    h_fwd = mlstm_chunkwise(q, k, v, gates[0, 0], gates[0, 1])
    flip = lambda t: jnp.flip(t, axis=2)
    h_bwd = flip(mlstm_chunkwise(flip(q), flip(k), flip(v),
                                 jnp.flip(gates[1, 0], -1), jnp.flip(gates[1, 1], -1)))
    h = h_fwd + h_bwd
    mu = h.mean(-1, keepdims=True)
    var = jnp.mean((h - mu) ** 2, axis=-1, keepdims=True)
    h = ((h - mu) * lax.rsqrt(var + EPS)).transpose(0, 2, 1, 3).reshape(B, S, MLSTM_W)
    h = h * norm_g.astype(jnp.float32) * jax.nn.sigmoid(o.astype(jnp.float32))
    return h.astype(z.dtype)

def diff_attention_branch(z, lam, norm_g, lam_init):
    B, S, _ = z.shape
    H = DIFF_HEADS
    q = z[..., OFF_DQ:OFF_DK].reshape(B, S, H, 2, DIFF_DH).transpose(0, 2, 3, 1, 4)
    k = z[..., OFF_DK:OFF_DV].reshape(B, S, H, 2, DIFF_DH).transpose(0, 2, 3, 1, 4)
    v = z[..., OFF_DV:OFF_GATE].reshape(B, S, H, DIFF_DV).transpose(0, 2, 1, 3)
    lamf = lam.astype(jnp.float32)
    lam_full = (jnp.exp(jnp.sum(lamf[0] * lamf[1])) - jnp.exp(jnp.sum(lamf[2] * lamf[3]))
                + lam_init)
    slopes = jnp.exp2(-8.0 * jnp.arange(1, H + 1, dtype=jnp.float32) / H)
    scale = DIFF_DH ** -0.5
    NB = S // Q_BLOCK
    qb = q.reshape(B, H, 2, NB, Q_BLOCK, DIFF_DH).transpose(3, 0, 1, 2, 4, 5)
    pos = jnp.arange(S, dtype=jnp.int32)

    def block(args):
        q_blk, start = args
        s = jnp.einsum('bhiqd,bhikd->bhiqk', q_blk, k).astype(jnp.float32) * scale
        tq = start + jnp.arange(Q_BLOCK, dtype=jnp.int32)
        dist = jnp.abs(tq[:, None] - pos[None, :]).astype(jnp.float32)
        s = s - (slopes[:, None, None] * dist)[None, :, None]
        p = jax.nn.softmax(s, axis=-1)
        a = p[:, :, 0] - lam_full * p[:, :, 1]
        return jnp.einsum('bhqk,bhkv->bhqv', a.astype(v.dtype), v)

    starts = jnp.arange(NB, dtype=jnp.int32) * Q_BLOCK
    o = lax.map(block, (qb, starts))
    o = o.transpose(1, 2, 0, 3, 4).reshape(B, H, S, DIFF_DV).astype(jnp.float32)
    o = o * lax.rsqrt(jnp.mean(o * o, axis=-1, keepdims=True) + EPS)
    o = o * norm_g.astype(jnp.float32) * (1.0 - lam_init)
    return o.transpose(0, 2, 1, 3).reshape(B, S, DIFF_W).astype(z.dtype)

def expert_choice_ffn(h, w_router, w_gate, w_up, w_down):
    B, S, _ = h.shape
    cap = EC_CAPACITY * S // N_EXPERTS
    aff = jax.nn.softmax(jnp.einsum('bsd,de->bse', h, w_router).astype(jnp.float32), axis=-1)
    g, idx = lax.top_k(aff.transpose(0, 2, 1), cap)
    bidx = jnp.arange(B)[:, None, None]
    xe = h[bidx, idx]
    hid = (jax.nn.silu(jnp.einsum('becd,edf->becf', xe, w_gate))
           * jnp.einsum('becd,edf->becf', xe, w_up))
    ye = jnp.einsum('becf,efd->becd', hid, w_down) * g[..., None].astype(h.dtype)
    return jnp.zeros_like(h).at[bidx, idx].add(ye)

def second_inputs(seed: int = 0) -> dict:
    key = jax.random.key(seed)
    ks = jax.random.split(key, 20)
    nrm = lambda k, shape, s: jax.random.normal(k, shape, jnp.float32) * s
    i_bias = nrm(ks[3], (DEPTH, 2, MLSTM_HEADS), 0.1)
    f_bias = jnp.linspace(3.0, 6.0, MLSTM_HEADS, dtype=jnp.float32) + nrm(ks[4], (DEPTH, 2, MLSTM_HEADS), 0.1)
    b_mgate = jnp.stack([i_bias, f_bias], axis=2).reshape(DEPTH, N_MGATES)
    return {
        "x": nrm(ks[0], (BATCH, SEQ, D_MODEL), 1.0),
        "norm_mix_g": 1.0 + nrm(ks[1], (DEPTH, D_MODEL), 0.01),
        "w_in": nrm(ks[2], (DEPTH, D_MODEL, IN_COLS), D_MODEL ** -0.5),
        "b_mgate": b_mgate,
        "conv_w": nrm(ks[5], (DEPTH, CONV_W, 2 * MLSTM_W), CONV_W ** -0.5),
        "conv_b": nrm(ks[6], (DEPTH, 2 * MLSTM_W), 0.01),
        "mlstm_norm_g": 1.0 + nrm(ks[7], (DEPTH, MLSTM_W), 0.01),
        "diff_lam": nrm(ks[8], (DEPTH, 4, DIFF_DH), 0.1),
        "diff_norm_g": 1.0 + nrm(ks[9], (DEPTH, DIFF_DV), 0.01),
        "w_up_a": nrm(ks[10], (DEPTH, MLSTM_W, D_MODEL), MLSTM_W ** -0.5),
        "w_up_b": nrm(ks[11], (DEPTH, DIFF_W, D_MODEL), DIFF_W ** -0.5),
        "w_out": nrm(ks[12], (DEPTH, D_MODEL, D_MODEL), D_MODEL ** -0.5),
        "norm_ffn_g": 1.0 + nrm(ks[13], (DEPTH, D_MODEL), 0.01),
        "w_router": nrm(ks[14], (DEPTH, D_MODEL, N_EXPERTS), D_MODEL ** -0.5),
        "w_gate_e": nrm(ks[15], (DEPTH, N_EXPERTS, D_MODEL, D_FF_EXPERT), D_MODEL ** -0.5),
        "w_up_e": nrm(ks[16], (DEPTH, N_EXPERTS, D_MODEL, D_FF_EXPERT), D_MODEL ** -0.5),
        "w_down_e": nrm(ks[17], (DEPTH, N_EXPERTS, D_FF_EXPERT, D_MODEL), D_FF_EXPERT ** -0.5),
        "norm_f_g": 1.0 + nrm(ks[18], (D_MODEL,), 0.01),
    }

def second_block(x, norm_mix_g, w_in, b_mgate, conv_w, conv_b, mlstm_norm_g, diff_lam, diff_norm_g,
              w_up_a, w_up_b, w_out, norm_ffn_g, w_router, w_gate_e, w_up_e, w_down_e, norm_f_g):
    for l in range(DEPTH):
        lam_init = 0.8 - 0.6 * math.exp(-0.3 * l)
        h = rms_norm(x, norm_mix_g[l])
        z = jnp.einsum('bsd,dc->bsc', h, w_in[l])
        y_a = jnp.einsum('bsw,wd->bsd', mlstm_branch(z, conv_w[l], conv_b[l], b_mgate[l], mlstm_norm_g[l]), w_up_a[l])
        y_b = jnp.einsum('bsw,wd->bsd', diff_attention_branch(z, diff_lam[l], diff_norm_g[l], lam_init), w_up_b[l])
        g_a = jax.nn.sigmoid(z[..., OFF_GATE:OFF_GATE + D_MODEL])
        g_b = jax.nn.sigmoid(z[..., OFF_GATE + D_MODEL:])
        x = x + jnp.einsum('bsd,de->bse', g_a * y_a + g_b * y_b, w_out[l])
        h2 = rms_norm(x, norm_ffn_g[l])
        x = x + expert_choice_ffn(h2, w_router[l], w_gate_e[l], w_up_e[l], w_down_e[l])
    return rms_norm(x, norm_f_g)


def setup_inputs(seed=0):
    out = dict(first_inputs(seed))
    for name, value in second_inputs(seed + 1).items():
        if name != "x":
            out[name + "_2"] = value
    return out


def reference(
    x, c, w_in, w_out, sinks, rel_bias, w_ada, b_ada, norm_gains, w1, b1, w2, b2, norm_mix_g_2,
    w_in_2, b_mgate_2, conv_w_2, conv_b_2, mlstm_norm_g_2, diff_lam_2, diff_norm_g_2, w_up_a_2,
    w_up_b_2, w_out_2, norm_ffn_g_2, w_router_2, w_gate_e_2, w_up_e_2, w_down_e_2, norm_f_g_2,
):
    x = first_block(
        x, c, w_in, w_out, sinks, rel_bias, w_ada, b_ada, norm_gains, w1, b1, w2, b2,
    )
    return second_block(
        x, norm_mix_g_2, w_in_2, b_mgate_2, conv_w_2, conv_b_2, mlstm_norm_g_2, diff_lam_2,
        diff_norm_g_2, w_up_a_2, w_up_b_2, w_out_2, norm_ffn_g_2, w_router_2, w_gate_e_2,
        w_up_e_2, w_down_e_2, norm_f_g_2,
    )


_drawn_inputs = setup_inputs


def setup_inputs(seed=0):
    import zlib

    import numpy as np

    out = dict(_drawn_inputs(seed))
    spreads = {}
    factors = {'sinks': 6.57,
     'b1': 4.704,
     'b2': 8.0,
     'norm_mix_g_2': 6.773,
     'conv_b_2': 8.0,
     'mlstm_norm_g_2': 8.0,
     'diff_lam_2': 5.033,
     'diff_norm_g_2': 8.0,
     'norm_ffn_g_2': 8.0,
     'norm_f_g_2': 5.704}
    for name, (base, spread) in spreads.items():
        noise = np.random.default_rng([zlib.crc32(name.encode()), seed]).standard_normal(out[name].shape)
        drawn = base * np.exp(spread * noise) if base else spread * noise
        out[name] = __import__('jax').numpy.asarray(drawn.astype(out[name].dtype))
    for name, factor in factors.items():
        out[name] = (out[name] * factor).astype(out[name].dtype)
    return out
```

```python
from contextlib import ExitStack
import math

import numpy as np

import concourse.bass as bass
from concourse import mybir

ALU = mybir.AluOpType
ACT = mybir.ActivationFunctionType
AX_X = mybir.AxisListType.X
F32 = mybir.dt.float32
BF16 = mybir.dt.bfloat16

P = 128
S = 256
D = 1024
NT = S // P
KD = D // P
HD = 64
HEADS = 16
BUCKETS = 32
W_A = 512
D_FF = 4096
MH = 4
MW = 512
EXPERTS = 16
CAP = 32
D_EXP = 2048
EPS = 1e-6
BIG = 3e38
MASKED = -1e30
LAM_INIT = 0.8 - 0.6 * math.exp(-0.3 * 0)
GATE0 = 2048
DIFF0 = GATE0 + 16

SLOT = 2048
RING = 12
N_ADA0, N_WIN, N_ADA12, N_WOUT, N_W1, N_W2, N_MIX2, N_GATES2, N_UP, N_WOUT2 = 8, 9, 16, 4, 16, 16, 14, 8, 4, 4
PRELUDE = N_ADA0 + N_WIN + N_ADA12 + N_WOUT + N_W1 + N_W2 + N_MIX2 + N_GATES2 + N_UP + N_WOUT2
PER_EXPERT = 24
assert PER_EXPERT % RING == 0
FIRST = -PRELUDE % RING
G_ADA0 = FIRST
G_WIN = G_ADA0 + N_ADA0
G_ADA12 = G_WIN + N_WIN
G_WOUT = G_ADA12 + N_ADA12
G_W1 = G_WOUT + N_WOUT
G_W2 = G_W1 + N_W1
G_MIX2 = G_W2 + N_W2
G_GATES2 = G_MIX2 + N_MIX2
G_UP = G_GATES2 + N_GATES2
G_WOUT2 = G_UP + N_UP
G_EXPERTS = G_WOUT2 + N_WOUT2
assert G_EXPERTS % RING == 0

C_IDENT = 0
C_SLOTCOL = C_IDENT + P
C_SLOTROW = C_SLOTCOL + 1
C_TIE = C_SLOTROW + CAP
C_KEEPF = C_TIE + P
C_KEEPB = C_KEEPF + S
C_DIST = C_KEEPB + S
C_ONEHOT = C_DIST + NT * S
C_MASK = C_ONEHOT + 384
C_END = C_MASK + 384

A_GAIN, A_BADA, A_B1, A_ROWS = 0, 32, 80, 112
B_CONVW, B_CONVB, B_NMIX, B_NFFN, B_MLN, B_DNG, B_C, B_ROWS = 0, 40, 48, 56, 64, 68, 69, 77


def shape_constants():
    c = np.zeros((P, C_END), np.float32)
    p = np.arange(P)
    c[:, C_IDENT:C_IDENT + P] = np.eye(P)
    c[:, C_SLOTCOL] = p % CAP
    c[:, C_SLOTROW:C_SLOTROW + CAP] = np.arange(CAP)
    c[:, C_TIE:C_TIE + P] = p[:, None] < p[None, :]
    lower = np.where(p[None, :] <= p[:, None], BIG, -BIG)
    c[:, C_KEEPF:C_KEEPF + P] = BIG
    c[:, C_KEEPF + P:C_KEEPF + S] = lower
    c[:, C_KEEPB:C_KEEPB + P] = lower.T
    c[:, C_KEEPB + P:C_KEEPB + S] = BIG
    for t in range(NT):
        c[:, C_DIST + t * S:C_DIST + (t + 1) * S] = np.abs(t * P + p[:, None] - np.arange(S)[None, :])
    dist = S - 1 - np.arange(383)
    n = np.maximum(dist, 0)
    half = BUCKETS // 2
    large = half + (np.log(np.maximum(n, 1).astype(np.float32) / half) / math.log(128 / half) * half).astype(np.int32)
    bucket = np.where(n < half, n, np.minimum(large, BUCKETS - 1))
    c[bucket, C_ONEHOT + np.arange(383)] = 1.0
    c[:8, C_MASK:C_MASK + 383] = np.where(dist < 0, MASKED, 0.0)
    c[8:16, C_MASK:C_MASK + 383] = np.where((dist < 0) | (dist >= 128), MASKED, 0.0)
    return c


def build_program(nc, A, out, bias_scratch):
    with ExitStack() as ctx:
        def sb(name, shape, dt=F32):
            return ctx.enter_context(nc.sbuf_tensor(name, shape, dt))

        def sems(text):
            return [ctx.enter_context(nc.semaphore(n)) for n in text.split()]

        ring = sb("ring", [P, RING, SLOT])
        const = sb("const", [P, C_END])
        ident = const[:, C_IDENT:C_IDENT + P]
        slotcol = const[:, C_SLOTCOL:C_SLOTCOL + 1]
        slotrow = const[:, C_SLOTROW:C_SLOTROW + CAP]
        tie = const[:, C_TIE:C_TIE + P]
        keepf = const[:, C_KEEPF:C_KEEPF + S]
        keepb = const[:, C_KEEPB:C_KEEPB + S]
        dist = const[:, C_DIST:C_DIST + NT * S]
        onehot = const[0:BUCKETS, C_ONEHOT:C_ONEHOT + 384]
        maskrow = const[0:HEADS, C_MASK:C_MASK + 384]
        xres = sb("xres", [P, NT, D])
        hT = sb("hT", [P, KD, S])
        ybuf = sb("ybuf", [P, NT, D])
        work = sb("work", [P, NT, D])
        cols = sb("cols", [P, A_ROWS + B_ROWS])
        colA = cols[:, 0:A_ROWS]
        colB = cols[:, A_ROWS:A_ROWS + B_ROWS]
        ones = sb("ones", [P, P])
        ones16 = sb("ones16", [P, P], BF16)
        stats = sb("stats", [P, 7, 8])
        crep = sb("crep", [P, KD, 32])
        cact = sb("cact", [P, KD])
        modcol = sb("modcol", [P, 3, 4, 4])
        fold = sb("fold", [P, 2, KD])
        sinkbc = sb("sinkbc", [P, 8])
        relb = sb("relb", [BUCKETS, HEADS])
        router = sb("router", [P, KD, EXPERTS])
        lambc = sb("lambc", [P, 4, HD])
        lam = sb("lam", [P, 8])
        mgate = sb("mgate", [P, KD, 16])
        bmg = sb("bmg", [36, 2])
        ARENA = 16896
        arena = sb("arena", [P, ARENA])

        def view(at, *shape):
            n = int(np.prod(shape))
            assert at + n <= ARENA, (at, shape)
            v = arena[:, at:at + n]
            if len(shape) == 2:
                v = v.rearrange("p (a b) -> p a b", a=shape[0])
            if len(shape) == 3:
                v = v.rearrange("p (a b c) -> p a b c", a=shape[0], b=shape[1])
            return v

        rowsA, rowsB = view(0, P)[0:A_ROWS, :], view(P, P)[0:B_ROWS, :]
        qkT = view(0, 14, S)
        v1 = view(3584, NT, 640)
        biasm = view(4864, HEADS, 384)
        ffT = view(0, D_FF // P, S)
        logits = view(11008, 2, 384)
        relu = view(11008, 2, 512)
        G1 = view(12032, D)
        G2 = view(13056, D)
        b2bc = view(14080, D)
        att_s = view(15104, HEADS, 8)
        modrow = view(15232, 3, 512)
        attT = hT
        probs = work[:, 0, 0:768].rearrange("p (b n) -> p b n", b=2)
        probsT = work[:, 1, 0:768].rearrange("p (b n) -> p b n", b=2)
        zpad = view(0, 8, S + 4)
        expo = view(0, 2, 1024)
        qkc = view(2080, 8, S)
        conv = view(4128, 2, S)
        vo = view(4640, NT, 2 * MW)
        dqk = view(6688, 8, S)
        dv = view(8736, NT, MW)
        gT = view(9760, 16, S)
        rows2 = view(13856, 8, S)
        comb = view(13856, NT, S)
        combT = view(14368, NT, S)
        rowcols = view(15904, 3, NT, 36)
        alibi = view(16128, NT, S)
        unit_s = view(16640, 8, 16)
        mv = view(16768, 16, 2)
        bn6 = view(16800, 16, 6)
        wgi = ybuf[:, 0, 0:KD * 36].rearrange("p (k m) -> p k m", k=KD)
        wgf = ybuf[:, 0, 512:512 + KD * 36].rearrange("p (k m) -> p k m", k=KD)
        mixin = ybuf
        xeT = view(0, KD, EXPERTS * CAP)
        selTg = view(4096, EXPERTS, S)
        affbc = view(8192, EXPERTS, S)
        sel = view(12288, NT, EXPERTS * CAP)
        beats = hT[:, :, :].rearrange("p k s -> p (k s)").bitcast(BF16).rearrange("p (i e t) -> p i e t", i=NT, e=8)
        beats_eq = view(13312, 1024).bitcast(BF16).rearrange("p (i e t) -> p i e t", i=NT, e=8)
        aff = view(14336, NT, EXPERTS)
        rankc = view(14368, NT, EXPERTS)
        aff_s = view(14400, 8)
        xe = view(14464, KD, CAP)
        selx = view(14720, S)
        gfinal = ybuf[:, 0, :]
        silu = view(8192, 512)
        hid = view(8704, 512)
        hidT = view(9216, 4, 4, CAP)
        ye = view(9728, 512)

        PS = ctx.enter_context(nc.psum_tensor("PS", [P, 8, 512], F32))

        loaded = [ctx.enter_context(nc.semaphore(f"loaded{i}")) for i in range(RING)]
        (slots_used, consts_in, x_in, rows_in, late_in, mg_in, ones_set, cols_turned, cols_set, bias_rows, bias_row_set,
         bias_stored, bias_in, bias_copied, c_acted, crep_set, bg_in, gfinal_in) = sems(
            "slots_used consts_in x_in rows_in late_in mg_in ones_set cols_turned cols_set bias_rows bias_row_set "
            "bias_stored bias_in bias_copied c_acted crep_set bg_in gfinal_in")
        modrow_set, mod_turned, modcol_set, folded, g_spread, g_ready = sems(
            "modrow_set mod_turned modcol_set folded g_spread g_ready")
        dve_chain, act_chain, pool_chain = sems("dve_chain act_chain pool_chain")
        win_out = sems("win_out_dve win_out_act")
        kswap_in, = sems("kswap_in")
        scored, logit_set, negmax_set, exp_set, probs_set, probs_turned, probsT_set, weighed, att_out = sems(
            "scored logit_set negmax_set exp_set probs_set probs_turned probsT_set weighed att_out")
        wout_out = sems("wout_out_dve wout_out_act")
        w1_relu, w1_out, w2_out, x1_set, x2_set, x3_set = sems("w1_relu w1_out w2_out x1_set x2_set x3_set")
        mix_out = sems("mix_out_dve mix_out_act")
        (gate_rows, gate_rows_set, gate_exp, gate_ln, gate_m, gate_em, gate_cols, gate_cols_set, pads_set, wg_set,
         bmg_set, conv_set, qk_set, lam_dots, lam_exps, lam_set) = sems(
            "gate_rows gate_rows_set gate_exp gate_ln gate_m gate_em gate_cols gate_cols_set pads_set wg_set "
            "bmg_set conv_set qk_set lam_dots lam_exps lam_set")
        (unit_scored, unit_read, unit_arg, unit_exp, unit_comb, unit_turned, unit_T, unit_out, raw_set, alibi_set,
         gates_out) = sems(
            "unit_scored unit_read unit_arg unit_exp unit_comb unit_turned unit_T unit_out raw_set alibi_set gates_out")
        osig_set, gsig_set, var2_set, root2_set, mixed = sems(
            "osig_set gsig_set var2_set root2_set mixed")
        (logit16, negmax16, exp16, aff_set, aff_spread, affbc_set, beats_set, rank_spread, rank_cols, selT_set, rankc_set,
         sel_set, gathered, xe_out, acc_started) = sems(
            "logit16 negmax16 exp16 aff_set aff_spread affbc_set beats_set rank_spread rank_cols selT_set rankc_set "
            "sel_set gathered xe_out acc_started")
        xe_ready, selx_ready, silu_set, hid_set, hid_turned, hidT_set, ye_set, scattered = sems(
            "xe_ready selx_ready silu_set hid_set hid_turned hidT_set ye_set scattered")
        final_copied, final_set, out_stored = sems("final_copied final_set out_stored")
        squared, variance_set, root_set = sems("squared variance_set root_set")
        N1, POST1, N2, POST2, N3, N4, NLAST = range(7)
        normed, turned, placed = sems("normed turned placed")
        T1, T2, T3, TBRANCH, T4 = range(5)

        def slot(g):
            return ring[:, g % RING, :]

        def loads_of(g):
            return g // RING + (1 if g % RING >= FIRST else 0)

        def arrived(eng, g):
            eng.wait_ge(loaded[g % RING], 16 * loads_of(g))

        def used(g):
            return g - FIRST + 1

        class Chain:
            def __init__(self, eng, sem):
                self.eng, self.sem, self.n = eng, sem, 0

            def __call__(self, instruction):
                self.n += 1
                instruction.then_inc(self.sem, 1)
                self.eng.wait_ge(self.sem, self.n)

        def qk_chunks(chunk):
            v = qkT[:, chunk:chunk + 2, :].rearrange("p m (t s) -> p (m t) s", t=NT)
            return v if chunk in (4, 6) else v[:, :, ::-1]

        def by_rows(w):
            return w.rearrange("(k p) n -> p k n", p=P)

        w_in, w_out, w_ada = by_rows(A["w_in"][0]), by_rows(A["w_out"][0]), A["w_ada"][0]
        w1, w2 = by_rows(A["w1"][0]), by_rows(A["w2"][0])
        w_in2, w_out2 = by_rows(A["w_in_2"][0]), by_rows(A["w_out_2"][0])
        up_a, up_b = by_rows(A["w_up_a_2"][0]), by_rows(A["w_up_b_2"][0])

        def k8(g):
            return slot(g).rearrange("p (k n) -> p k n", k=KD)

        loads = []
        for k in range(8):
            loads.append((slot, w_ada[k * P:(k + 1) * P, 0:SLOT]))
        for i in range(N_WIN):
            loads.append((k8, w_in[:, :, 256 * i:256 * (i + 1)]))
        for r in (1, 2):
            for k in range(8):
                loads.append((slot, w_ada[k * P:(k + 1) * P, r * SLOT:(r + 1) * SLOT]))
        for i in range(N_WOUT):
            loads.append((k8, w_out[:, :, 256 * i:256 * (i + 1)]))
        for i in range(N_W1):
            loads.append((k8, w1[:, :, 256 * i:256 * (i + 1)]))
        for i in range(N_W2):
            loads.append((lambda g: slot(g).rearrange("p (k n) -> p k n", k=2), w2[:, 2 * i:2 * i + 2, :]))
        mix_cols = [256 * i for i in range(6)] + [DIFF0 + 256 * i for i in range(6)] + [1536, 1792]
        gate_cols0 = DIFF0 + 3 * MW
        for c in mix_cols + [gate_cols0 + 256 * i for i in range(N_GATES2)]:
            loads.append((k8, w_in2[:, :, c:c + 256]))
        for half in range(2):
            for w in (up_a, up_b):
                loads.append((lambda g: slot(g).rearrange("p (k n) -> p k n", k=4), w[:, :, 512 * half:512 * half + 512]))
        for i in range(N_WOUT2):
            loads.append((k8, w_out2[:, :, 256 * i:256 * (i + 1)]))
        assert len(loads) == PRELUDE

        block = ctx.enter_context(nc.Block())

        @block.sync
        def _(sp):
            for n, (dst, src) in enumerate(loads):
                g = FIRST + n
                if n >= RING:
                    sp.wait_ge(slots_used, used(g - RING))
                sp.dma_start(dst(g), src).then_inc(loaded[g % RING], 16)
            wg, wu, wd = A["w_gate_e_2"], A["w_up_e_2"], A["w_down_e_2"]
            wg_rows = wg.rearrange("l e (k p) n -> (l e k) p n", p=P)
            wu_rows = wu.rearrange("l e (k p) n -> (l e k) p n", p=P)
            wd_rows = wd.rearrange("l e (k p) n -> (l e k) p n", p=P)
            with sp.Fori(0, EXPERTS) as e:
                for r in range(PER_EXPERT):
                    sp.wait_ge(slots_used, e * PER_EXPERT + used(G_EXPERTS + r - RING))
                    if r < 16:
                        rows = (wg_rows, wu_rows)[r // 8]
                        src = rows[bass.ds(e * 8 + r % 8, 1), :, :].rearrange("o p n -> p (o n)")
                        dst = ring[:, r % RING, :]
                    else:
                        src = wd_rows[bass.ds(e * 16 + 2 * (r - 16), 2), :, :].rearrange("o p n -> p o n")
                        dst = ring[:, r % RING, :].rearrange("p (o n) -> p o n", o=2)
                    sp.dma_start(dst, src).then_inc(loaded[r % RING], 16)
            for t in range(NT):
                sp.wait_ge(final_set, t + 1)
                sp.dma_start(out[0, t * P:(t + 1) * P, :], work[:, t, :]).then_inc(out_stored, 16)
            sp.wait_ge(out_stored, 16 * NT)

        @block.tensor
        def _(pe):
            def turn(out_, in_, n=P):
                return nc.tensor.transpose(out_, in_, ident[0:n, 0:n])

            def weights_still(g, bank, actT):
                w = k8(g)
                arrived(pe, g)
                for m in range(2):
                    for k in range(KD):
                        mm = nc.tensor.matmul(PS[:, bank, m * S:(m + 1) * S], w[:, k, m * P:(m + 1) * P],
                                              actT[:, k, :], start=(k == 0), stop=(k == KD - 1))
                mm.then_inc(slots_used, 1)

            def tokens_still(g, bank, actT):
                w = k8(g)
                arrived(pe, g)
                for t in range(NT):
                    for k in range(KD):
                        mm = nc.tensor.matmul(PS[:, bank, t * 256:(t + 1) * 256], actT[:, k, t * P:(t + 1) * P],
                                              w[:, k, :], start=(k == 0), stop=(k == KD - 1))
                mm.then_inc(slots_used, 1)

            def turn_tiles(n, src, base):
                for t in range(NT):
                    pe.wait_ge(normed, 2 * n + t + 1)
                    for k in range(KD):
                        mm = turn(PS[:, base + 2 * t + k // 4, (k % 4) * P:(k % 4 + 1) * P],
                                  src[:, t, k * P:(k + 1) * P])
                        if k % 4 == 3:
                            mm.then_inc(turned, 1)

            pe.wait_ge(consts_in, 16)
            pe.wait_ge(rows_in, 16 * 10)
            turn(PS[:, 0, 0:A_ROWS], rowsA[:, :], A_ROWS)
            turn(PS[:, 0, A_ROWS:A_ROWS + B_ROWS], rowsB[:, :], B_ROWS).then_inc(cols_turned, 1)
            pe.wait_ge(late_in, 16 * 7)
            nc.tensor.matmul(PS[0:HEADS, 1, 0:384], relb[:, :], onehot, start=True, stop=True).then_inc(bias_rows, 1)

            def ada(g, k, bank):
                arrived(pe, g)
                for j in range(4):
                    mm = nc.tensor.matmul(PS[32 * j:32 * j + 32, bank, :], crep[:, k, :],
                                          slot(g)[:, 512 * j:512 * (j + 1)], start=(k == 0), stop=(k == 7),
                                          tile_position=(0, 32 * j))
                mm.then_inc(slots_used, 1)

            def turn_mod(r, bank):
                for q in range(4):
                    mm = turn(PS[:, bank, q * P:(q + 1) * P], modrow[:, r, q * P:(q + 1) * P])
                mm.then_inc(mod_turned, 1)

            pe.wait_ge(crep_set, 1)
            for k in range(8):
                ada(G_ADA0 + k, k, 2)
            pe.wait_ge(modrow_set, 1)
            turn_mod(0, 3)
            turn_tiles(T1, work, 4)
            pe.wait_ge(placed, 4 * T1 + 4)
            pe.wait_ge(bias_row_set, 1)
            for i in range(N_WIN):
                if i >= 4:
                    pe.wait_ge(win_out[i % 2], (i - 4) // 2 + 1)
                g = G_WIN + i
                if i in (2 * 2, 2 * 2 + 1):
                    tokens_still(g, i % 4, hT)
                elif i < 8:
                    weights_still(g, i % 4, hT)
                else:
                    w = k8(g)
                    arrived(pe, g)
                    for k in range(KD):
                        nc.tensor.matmul(PS[:, 0, 0:S], w[:, k, 0:P], hT[:, k, :], start=(k == 0), stop=(k == KD - 1))
                    for t in range(NT):
                        for k in range(KD):
                            mm = nc.tensor.matmul(PS[:, 0, S + t * P:S + (t + 1) * P], hT[:, k, t * P:(t + 1) * P],
                                                  w[:, k, P:2 * P], start=(k == 0), stop=(k == KD - 1))
                    mm.then_inc(slots_used, 1)

            def heads_qkv(h):
                if h < 8:
                    r = 64 * (h % 2)
                    return r, qkT[r:r + HD, h // 2, :], qkT[r:r + HD, 4 + h // 2, :], h * HD
                j = h - 8
                r = 64 * (j % 2)
                kv = j // 4
                kchunk = 12 if kv == j % 2 else 13
                return r, qkT[r:r + HD, 8 + j // 2, :], qkT[r:r + HD, kchunk, :], W_A + kv * HD

            def score(h):
                r, q, k, _ = heads_qkv(h)
                if h == 8:
                    pe.wait_ge(kswap_in, 32)
                if h >= 2:
                    pe.wait_ge(logit_set, h - 1)
                nc.tensor.matmul(PS[:, h % 2, 0:S], q[:, P:S], k[:, :], start=True, stop=True)
                nc.tensor.matmul(PS[:, h % 2, S:S + P], q[:, 0:P], k[:, 0:P], start=True, stop=True)\
                    .then_inc(scored, 1)

            def turn_probs(h):
                pe.wait_ge(probs_set, h + 1)
                if h >= 2:
                    pe.wait_ge(probsT_set, h - 1)
                b = 2 + h % 2
                turn(PS[:, b, 0:P], probs[:, h % 2, S:S + P])
                turn(PS[:, b, P:S], probs[:, h % 2, 0:P])
                turn(PS[:, b, S:S + P], probs[:, h % 2, P:S]).then_inc(probs_turned, 1)

            def weigh(h):
                r, _, _, c = heads_qkv(h)
                pe.wait_ge(probsT_set, h + 1)
                if h % 2 == 0 and h >= 4:
                    pe.wait_ge(att_out, h // 2 - 1)
                o = PS[r:r + HD, 4 + (h // 2) % 2, :]
                nc.tensor.matmul(o[:, 0:S], v1[:, 0, c:c + HD], probsT[:, h % 2, 0:S], start=True, stop=False)
                nc.tensor.matmul(o[:, P:S], v1[:, 1, c:c + HD], probsT[:, h % 2, S:S + P], start=False, stop=True)\
                    .then_inc(weighed, 1)

            pe.wait_ge(win_out[0], 5)
            pe.wait_ge(win_out[1], 4)
            for h in range(HEADS + 2):
                if h < HEADS:
                    score(h)
                    ada(G_ADA12 + h, h % 8, 6 + h // 8)
                if 1 <= h <= HEADS:
                    turn_probs(h - 1)
                if h >= 2:
                    weigh(h - 2)
            pe.wait_ge(modrow_set, 3)
            pe.wait_ge(logit_set, HEADS)
            turn_mod(1, 0)
            turn_mod(2, 1)
            pe.wait_ge(probsT_set, HEADS)
            for n, (r, j, bank) in enumerate([(1, 0, 2), (1, 1, 3), (2, 2, 6), (2, 3, 7)]):
                nc.tensor.matmul(PS[:, bank, :], ones[32 * j:32 * j + 1, :], modrow[32 * j:32 * j + 1, r, :],
                                 start=True, stop=True, tile_position=(32 * j, 0)).then_inc(g_spread, 1)
            pe.wait_ge(att_out, HEADS // 2)
            pe.wait_ge(modcol_set, 3)
            pe.wait_ge(g_ready, 4)
            for i in range(N_WOUT):
                tokens_still(G_WOUT + i, i, attT)

            turn_tiles(T2, work, 4)
            pe.wait_ge(placed, 4 * T2 + 4)
            for i in range(N_W1):
                if i >= 4:
                    pe.wait_ge(w1_relu, 2 * (i - 3))
                weights_still(G_W1 + i, i % 4, hT)
            for i in range(N_W2):
                pe.wait_ge(w1_out, i + 1)
                w = slot(G_W2 + i).rearrange("p (k n) -> p k n", k=2)
                arrived(pe, G_W2 + i)
                for a in range(2):
                    for t in range(NT):
                        for half in range(2):
                            mm = nc.tensor.matmul(PS[:, 4 + 2 * t + half, :], ffT[:, 2 * i + a, t * P:(t + 1) * P],
                                                  w[:, a, 512 * half:512 * (half + 1)],
                                                  start=(i == 0 and a == 0), stop=(i == N_W2 - 1 and a == 1))
                mm.then_inc(slots_used, 1)

            turn_tiles(T3, work, 0)
            pe.wait_ge(placed, 4 * T3 + 4)
            pe.wait_ge(wg_set, 4)
            for part, w in enumerate((wgi, wgf)):
                for k in range(KD):
                    mm = nc.tensor.matmul(PS[0:36, 4, part * S:(part + 1) * S], w[:, k, :], hT[:, k, :],
                                          start=(k == 0), stop=(k == KD - 1))
            mm.then_inc(gate_rows, 1)
            for i in range(N_MIX2):
                if i >= 4:
                    pe.wait_ge(mix_out[i % 2], (i - 4) // 2 + 1)
                if i in (4, 5, 10, 11, 12, 13):
                    tokens_still(G_MIX2 + i, i % 4, hT)
                else:
                    weights_still(G_MIX2 + i, i % 4, hT)
                if i == 8:
                    pe.wait_ge(gate_em, 1)
                    for n, row in enumerate((4, 5, 7)):
                        for t in range(NT):
                            mm = turn(PS[:, 5, (2 * n + t) * 36:(2 * n + t + 1) * 36],
                                      rows2[0:36, row, t * P:(t + 1) * P], 36)
                    mm.then_inc(gate_cols, 1)

            def unit_scores(u):
                b = 2 * (u % 2)
                if u >= 2:
                    pe.wait_ge(unit_read, u - 1)
                if u < MH:
                    for t in range(NT):
                        nc.tensor.matmul(PS[:, b, t * S:(t + 1) * S], qkc[:, u, t * P:(t + 1) * P], qkc[:, 4 + u, :],
                                         start=True, stop=True)
                    for d in range(2):
                        for t in range(NT):
                            c = rowcols[:, 0, t, 32 * d + u:32 * d + u + 1]
                            mm = turn(PS[:, b + 1, d * S + t * P:d * S + (t + 1) * P], c.to_broadcast([P, P]))
                else:
                    h = u - MH
                    for t in range(NT):
                        for c in range(2):
                            mm = nc.tensor.matmul(PS[:, b + c, t * S:(t + 1) * S],
                                                  dqk[64 * c:64 * c + HD, h, t * P:(t + 1) * P],
                                                  dqk[64 * c:64 * c + HD, 4 + h, :], start=True, stop=True)
                mm.then_inc(unit_scored, 1)

            def unit_tail(u):
                pe.wait_ge(unit_comb, u + 1)
                if u >= 1:
                    pe.wait_ge(unit_T, u)
                for j in range(NT):
                    for t in range(NT):
                        mm = turn(PS[:, 4, j * S + t * P:j * S + (t + 1) * P], comb[:, t, j * P:(j + 1) * P])
                mm.then_inc(unit_turned, 1)
                pe.wait_ge(unit_T, u + 1)
                if u >= 1:
                    pe.wait_ge(raw_set, u)
                v = vo if u < MH else dv
                c = (u % MH) * P
                for t in range(NT):
                    for j in range(NT):
                        mm = nc.tensor.matmul(PS[:, 5, t * P:(t + 1) * P], combT[:, j, t * P:(t + 1) * P],
                                              v[:, j, c:c + P], start=(j == 0), stop=(j == NT - 1))
                mm.then_inc(unit_out, 1)

            pe.wait_ge(mix_out[0], N_MIX2 // 2)
            pe.wait_ge(mix_out[1], N_MIX2 // 2)
            pe.wait_ge(qk_set, 8)
            pe.wait_ge(gate_cols_set, 1)
            unit_scores(0)
            for u in range(2 * MH):
                if u + 1 < 2 * MH:
                    unit_scores(u + 1)
                if u >= 2:
                    pe.wait_ge(gates_out, u - 1)
                weights_still(G_GATES2 + u, 6 + u % 2, hT)
                unit_tail(u)

            turn_tiles(TBRANCH, work, 0)
            pe.wait_ge(placed, 4 * TBRANCH + 4)
            pe.wait_ge(raw_set, 8)
            pe.wait_ge(gates_out, 8)
            for i in range(N_UP):
                w = slot(G_UP + i).rearrange("p (k n) -> p k n", k=4)
                arrived(pe, G_UP + i)
                src = mixin[:, :, :].rearrange("p t d -> p (t d)").rearrange("p (k s) -> p k s", k=KD)
                for m in range(4):
                    for k in range(4):
                        mm = nc.tensor.matmul(PS[:, 2 * i + m // 2, (m % 2) * S:(m % 2 + 1) * S],
                                              w[:, k, m * P:(m + 1) * P], src[:, 4 * (i % 2) + k, :],
                                              start=(k == 0), stop=(k == 3))
                mm.then_inc(slots_used, 1)
            pe.wait_ge(mixed, 2)
            for i in range(N_WOUT2):
                tokens_still(G_WOUT2 + i, i, hT)

            turn_tiles(T4, work, 4)
            pe.wait_ge(placed, 4 * T4 + 4)
            for t in range(NT):
                for k in range(KD):
                    mm = nc.tensor.matmul(PS[:, 0, t * EXPERTS:(t + 1) * EXPERTS], hT[:, k, t * P:(t + 1) * P],
                                          router[:, k, :], start=(k == 0), stop=(k == KD - 1))
            mm.then_inc(logit16, 1)
            pe.wait_ge(aff_set, 1)

            def spread(q):
                if q >= 2:
                    pe.wait_ge(affbc_set, q - 1)
                for e in range(4):
                    for t in range(NT):
                        mm = turn(PS[:, 2 * (q % 2) + e // 2, (e % 2) * S + t * P:(e % 2) * S + (t + 1) * P],
                                  aff[:, t, 4 * q + e:4 * q + e + 1].to_broadcast([P, P]))
                mm.then_inc(aff_spread, 1)

            def count(q):
                e0 = 2 * (q % 4)
                bank = 4 + q % 2
                if q >= 2:
                    pe.wait_ge(selT_set, q - 1)
                for i in range(NT):
                    nc.tensor.matmul(PS[:, bank, :], ones16[:, :], beats[:, i, e0:e0 + 2, :].rearrange("p e t -> p (e t)"),
                                     start=(i == 0), stop=False, skip_group_check=True)
                o = PS[:, bank, :].rearrange("p (e t) -> p e t", e=2)
                for i in range(NT):
                    mm = nc.tensor.matmul(o[:, :, i * P:(i + 1) * P], ones16[:, :], beats_eq[:, i, e0:e0 + 2, :],
                                          start=False, stop=(i == NT - 1), skip_group_check=True)
                mm.then_inc(rank_spread, 1)
                for e in range(2):
                    for t in range(NT):
                        o = PS[:, 6, t * EXPERTS + 2 * q + e:t * EXPERTS + 2 * q + e + 1]
                        for i in range(NT):
                            nc.tensor.matmul(o, beats[:, i, e0 + e, t * P:(t + 1) * P], ones16[:, 0:1],
                                             start=(i == 0), stop=False)
                        mm = nc.tensor.matmul(o, beats_eq[:, t, e0 + e, :], ones16[:, 0:1], start=False, stop=True)
                mm.then_inc(rank_cols, 1)

            spread(0)
            for q in range(4):
                if q + 1 < 4:
                    spread(q + 1)
                pe.wait_ge(beats_set, q + 1)
                count(2 * q)
                count(2 * q + 1)
            pe.wait_ge(sel_set, 2)
            pe.wait_ge(affbc_set, 4)
            for k in range(KD):
                if k >= 4:
                    pe.wait_ge(xe_out, k - 3)
                for t in range(NT):
                    mm = nc.tensor.matmul(PS[:, k % 4, :], work[:, t, k * P:(k + 1) * P], sel[:, t, :],
                                          start=(t == 0), stop=(t == NT - 1))
                mm.then_inc(gathered, 1)
            pe.wait_ge(selT_set, 8)
            pe.wait_ge(rankc_set, 1)
            for t in range(NT):
                for half in range(2):
                    mm = nc.tensor.matmul(PS[:, 4 + 2 * t + half, :], ident, xres[:, t, 512 * half:512 * (half + 1)],
                                          start=True, stop=False, skip_group_check=True)
            mm.then_inc(scattered, 1)
            pe.wait_ge(xe_out, KD)

            with pe.Fori(0, EXPERTS) as e:
                pe.wait_ge(xe_ready, e + 1)
                for r in range(16):
                    g = G_EXPERTS + r
                    pe.wait_ge(loaded[r % RING], e * 32 + 16 * loads_of(g))
                    for j in range(4):
                        mm = nc.tensor.matmul(PS[32 * j:32 * j + 32, r // 8, :], xe[:, r % 8, :],
                                              slot(g)[:, 512 * j:512 * (j + 1)], start=(r % 8 == 0),
                                              stop=(r % 8 == 7), tile_position=(0, 32 * j))
                    mm.then_inc(slots_used, 1)
                pe.wait_ge(hid_set, e + 1)
                for c in range(4):
                    mm = turn(PS[:, 2, c * P:(c + 1) * P], hid[:, c * P:(c + 1) * P])
                mm.then_inc(hid_turned, 1)
                pe.wait_ge(hidT_set, e + 1)
                for r in range(16, 24):
                    g = G_EXPERTS + r
                    pe.wait_ge(loaded[r % RING], e * 32 + 16 * loads_of(g))
                    w = slot(g).rearrange("p (a n) -> p a n", a=2)
                    for half in range(2):
                        for a in range(2):
                            chunk = 2 * (r - 16) + a
                            q = 2 * half + a
                            mm = nc.tensor.matmul(PS[32 * q:32 * q + 32, 3, :], hidT[:, chunk % 4, chunk // 4, :],
                                                  w[:, a, 512 * half:512 * (half + 1)], start=(r == 16),
                                                  stop=(r == 23), tile_position=(0, 32 * q))
                    mm.then_inc(slots_used, 1)
                pe.wait_ge(selx_ready, e + 1)
                pe.wait_ge(ye_set, e + 1)
                for t in range(NT):
                    for half in range(2):
                        mm = nc.tensor.matmul(PS[:, 4 + 2 * t + half, :], selx[64 * half:64 * half + 64, t * P:(t + 1) * P],
                                              ye[64 * half:64 * half + 64, :], start=False, stop=False,
                                              skip_group_check=True, tile_position=(64 * half, 0))
                mm.then_inc(scattered, 1)

        @block.vector
        def _(dve):
            V = nc.vector
            then = Chain(dve, dve_chain)

            def variance(n):
                dve.wait_ge(squared, 2 * n + 2)
                V.tensor_scalar(stats[:, n, 2:4], stats[:, n, 0:2], 1.0 / D, EPS, ALU.mult, ALU.add)\
                    .then_inc(variance_set, 1)
                dve.wait_ge(root_set, n + 1)
                then(V.reciprocal(stats[:, n, 6:8], stats[:, n, 4:6]))

            def norm(n):
                variance(n)
                for t in range(NT):
                    V.tensor_scalar(work[:, t, :], xres[:, t, :], stats[:, n, 6 + t:7 + t], None, ALU.mult)\
                        .then_inc(normed, 1)

            def place(n, base, dst, scale, shift):
                for j in (0, 2):
                    dve.wait_ge(turned, 4 * n + j + 1)
                    for q in range(4):
                        k = 4 * (j % 2) + q
                        o, i = dst[:, k, (j // 2) * P:(j // 2 + 1) * P], PS[:, base + j, q * P:(q + 1) * P]
                        if shift is None:
                            last = V.tensor_scalar(o, i, scale(k), None, ALU.mult)
                        else:
                            last = V.tensor_scalar(o, i, scale(k), shift(k), ALU.mult, ALU.add)
                    last.then_inc(placed, 1)

            V.memset(ones[:, :], 1.0).then_inc(ones_set, 1)
            V.memset(ones16[:, :], 1.0).then_inc(ones_set, 1)
            V.memset(bmg[:, :], 0.0).then_inc(bmg_set, 1)
            dve.wait_ge(cols_turned, 1)
            V.tensor_copy(cols[:, :], PS[:, 0, 0:A_ROWS + B_ROWS]).then_inc(cols_set, 1)
            dve.wait_ge(bias_rows, 1)
            V.tensor_tensor(logits[0:HEADS, 0, :], PS[0:HEADS, 1, 0:384], maskrow, ALU.add).then_inc(bias_row_set, 1)
            dve.wait_ge(c_acted, 1)
            V.tensor_copy(crep[:, :, :], cact[:, :].unsqueeze(2).to_broadcast([P, KD, 32])).then_inc(crep_set, 1)

            norm(N1)

            def mod_columns(r, bank):
                dve.wait_ge(mod_turned, r + 1)
                V.tensor_tensor(modcol[:, r, :, :], PS[:, bank, :].rearrange("p (q j i) -> p j q i", q=4, j=4)[:, :, :, 0],
                                colA[:, A_BADA + 16 * r:A_BADA + 16 * (r + 1)].rearrange("p (j q) -> p j q", j=4),
                                ALU.add).then_inc(modcol_set, 1)
                dve.wait_ge(modcol_set, r + 1)

            def fold_gain(n, gain, scale):
                then(V.tensor_scalar(fold[:, n, :], scale, 1.0, None, ALU.add))
                V.tensor_tensor(fold[:, n, :], fold[:, n, :], colA[:, A_GAIN + 8 * gain:A_GAIN + 8 * gain + 8], ALU.mult)\
                    .then_inc(folded, 1)
                dve.wait_ge(folded, n + 1)

            dve.wait_ge(slots_used, used(G_ADA0 + 7))
            V.tensor_copy(modrow[:, 0, :], PS[:, 2, :]).then_inc(modrow_set, 1)
            mod_columns(0, 3)
            shift1 = modcol[:, 0, 0:2, :].rearrange("p j q -> p (j q)")
            scale1 = modcol[:, 0, 2:4, :].rearrange("p j q -> p (j q)")
            fold_gain(0, 0, scale1)
            place(T1, 4, hT, lambda k: fold[:, 0, k:k + 1], lambda k: shift1[:, k:k + 1])

            for i in range(0, N_WIN, 2):
                dve.wait_ge(slots_used, used(G_WIN + i))
                if i < 8:
                    if i == 4:
                        V.tensor_copy(v1[:, :, 0:256], PS[:, i % 4, :].rearrange("p (t n) -> p t n", t=NT))\
                            .then_inc(win_out[0], 1)
                    else:
                        chunk = {0: 0, 2: 4, 6: 8}[i]
                        V.tensor_copy(qk_chunks(chunk), PS[:, i % 4, :].rearrange("p (m s) -> p m s", m=4))\
                            .then_inc(win_out[0], 1)
                else:
                    V.tensor_copy(qkT[:, 12, :], PS[:, 0, 0:S])
                    V.tensor_copy(v1[:, :, W_A:W_A + P], PS[:, 0, S:2 * S].rearrange("p (t n) -> p t n", t=NT))\
                        .then_inc(win_out[0], 1)

            dve.wait_ge(bias_copied, 1)
            for h in range(HEADS + 1):
                if h < HEADS:
                    s = att_s[:, h, :]
                    L = logits[:, h % 2, :]
                    dve.wait_ge(scored, h + 1)
                    if h >= 2:
                        dve.wait_ge(exp_set, h - 1)
                    V.scalar_tensor_tensor(L, PS[:, h % 2, 0:384], HD ** -0.5, biasm[:, h, :], ALU.mult, ALU.add)\
                        .then_inc(logit_set, 1)
                    dve.wait_ge(logit_set, h + 1)
                    V.tensor_reduce(s[:, 0:1], L[:, 0:S], AX_X, ALU.max)
                    then(V.tensor_reduce(s[:, 1:2], L[:, S:384], AX_X, ALU.max))
                    sink = sinkbc[:, h - 8:h - 7] if h >= 8 else -BIG
                    V.tensor_scalar(s[:, 0:2], s[:, 0:2], sink, -1.0, ALU.max, ALU.mult).then_inc(negmax_set, 1)
                if h >= 1:
                    g = h - 1
                    s = att_s[:, g, :]
                    dve.wait_ge(exp_set, g + 1)
                    if g >= 8:
                        then(V.tensor_tensor(s[:, 2:4], s[:, 2:4], s[:, 4:6], ALU.add))
                    then(V.reciprocal(s[:, 6:8], s[:, 2:4]))
                    V.tensor_scalar(probs[:, g % 2, 0:S], probs[:, g % 2, 0:S], s[:, 6:7], None, ALU.mult)
                    V.tensor_scalar(probs[:, g % 2, S:384], probs[:, g % 2, S:384], s[:, 7:8], None, ALU.mult)\
                        .then_inc(probs_set, 1)
                    if g == 7:
                        dve.wait_ge(slots_used, used(G_ADA12 + 7))
                        V.tensor_copy(modrow[:, 1, :], PS[:, 6, :]).then_inc(modrow_set, 1)
            dve.wait_ge(slots_used, used(G_ADA12 + 15))
            V.tensor_copy(modrow[:, 2, :], PS[:, 7, :]).then_inc(modrow_set, 1)
            mod_columns(1, 0)
            mod_columns(2, 1)
            fold_gain(1, 2, modcol[:, 2, 0:2, :].rearrange("p j q -> p (j q)"))
            dve.wait_ge(bg_in, 16 * 2)
            for n, bank in enumerate((2, 3, 6, 7)):
                half = slice(512 * (n % 2), 512 * (n % 2) + 512)
                G, bg = (G1, G2)[n // 2], ybuf[:, n // 2, half]
                dve.wait_ge(g_spread, n + 1)
                then(V.tensor_tensor(bg, PS[:, bank, :], bg, ALU.add))
                V.tensor_tensor(G[:, half], G[:, half], bg, ALU.mult).then_inc(g_ready, 1)
            dve.wait_ge(g_ready, 4)

            def post_norm(n, G, done):
                variance(n)
                for t in range(NT):
                    then(V.scalar_tensor_tensor(work[:, t, :], ybuf[:, t, :], stats[:, n, 6 + t:7 + t], G, ALU.mult,
                                                ALU.mult))
                    V.tensor_tensor(xres[:, t, :], xres[:, t, :], work[:, t, :], ALU.add).then_inc(done, 1)

            for i in (0, 2):
                dve.wait_ge(slots_used, used(G_WOUT + i))
                V.tensor_copy(ybuf[:, :, 256 * i:256 * (i + 1)], PS[:, i, :].rearrange("p (t n) -> p t n", t=NT))\
                    .then_inc(wout_out[0], 1)
            post_norm(POST1, G1, x1_set)
            dve.wait_ge(x1_set, 2)
            norm(N2)
            shift2 = modcol[:, 1, 2:4, :].rearrange("p j q -> p (j q)")
            place(T2, 4, hT, lambda k: fold[:, 1, k:k + 1], lambda k: shift2[:, k:k + 1])
            for i in range(N_W1):
                dve.wait_ge(slots_used, used(G_W1 + i))
                if i >= 2:
                    dve.wait_ge(w1_out, i - 1)
                for m in range(2):
                    c = 2 * i + m
                    V.tensor_scalar(relu[:, i % 2, m * S:(m + 1) * S], PS[:, i % 4, m * S:(m + 1) * S],
                                    colA[:, A_B1 + c:A_B1 + c + 1], 0.0, ALU.add, ALU.max).then_inc(w1_relu, 1)
            dve.wait_ge(slots_used, used(G_W2 + N_W2 - 1))
            for t in range(NT):
                V.tensor_tensor(ybuf[:, t, :], PS[:, 4 + 2 * t:6 + 2 * t, :].rearrange("p b n -> p (b n)"), b2bc, ALU.add)\
                    .then_inc(w2_out, 1)
            post_norm(POST2, G2, x2_set)
            dve.wait_ge(x2_set, 2)
            norm(N3)
            place(T3, 0, hT, lambda k: colB[:, B_NMIX + k:B_NMIX + k + 1], None)

            def gate_rows_program():
                R = rows2[0:36, :, :]
                dve.wait_ge(gate_rows, 1)
                dve.wait_ge(mg_in, 16 * 5)
                dve.wait_ge(pads_set, 2)
                V.tensor_scalar(R[:, 0, :], PS[0:36, 4, 0:S], bmg[:, 0:1], None, ALU.add)
                then(V.tensor_scalar(R[:, 1, :], PS[0:36, 4, S:2 * S], bmg[:, 1:2], None, ALU.add))
                V.scalar_tensor_tensor(R[:, 2, :], R[:, 1, :], -1.0, R[:, 1, :], ALU.mult, ALU.min).then_inc(gate_rows_set, 1)
                dve.wait_ge(gate_ln, 1)
                then(V.scalar_tensor_tensor(R[:, 2, :], R[:, 1, :], 0.0, R[:, 2, :], ALU.min, ALU.subtract))
                zero = R[:, 6, :]
                for part, way in ((0, 1), (32, -1)):
                    r = rows2[part:part + 4, :, :]
                    ze = zero[part:part + 4, :]
                    then(V.tensor_tensor_scan(r[:, 3, ::way], r[:, 2, ::way], ze, 0.0, ALU.add, ALU.add))
                    then(V.tensor_tensor(r[:, 4, :], r[:, 0, :], r[:, 3, :], ALU.subtract))
                    then(V.tensor_tensor_scan(r[:, 5, ::way], r[:, 4, ::way], ze, 0.0, ALU.max, ALU.add))
                    V.tensor_tensor(r[:, 7, :], r[:, 3, :], r[:, 5, :], ALU.add).then_inc(gate_m, 1)

            def convolve(c):
                if c >= 2:
                    dve.wait_ge(qk_set, c - 1)
                a = conv[:, c % 2, :]
                then(V.tensor_scalar(a, zpad[:, c, 0:S], colB[:, B_CONVW + c:B_CONVW + c + 1],
                                     colB[:, B_CONVB + c:B_CONVB + c + 1], ALU.mult, ALU.add))
                for j in range(1, 5):
                    w = colB[:, B_CONVW + 8 * j + c:B_CONVW + 8 * j + c + 1]
                    ins = V.scalar_tensor_tensor(a, zpad[:, c, j:j + S], w, a, ALU.mult, ALU.add)
                    if j < 4:
                        then(ins)
                ins.then_inc(conv_set, 1)

            for i in range(0, N_MIX2, 2):
                dve.wait_ge(slots_used, used(G_MIX2 + i))
                turned_ = PS[:, i % 4, :].rearrange("p (m s) -> p m s", m=2)
                tokens_ = PS[:, i % 4, :].rearrange("p (t n) -> p t n", t=NT)
                if i == 0:
                    dve.wait_ge(pads_set, 2)
                if i < 4:
                    last = V.tensor_copy(zpad[:, 2 * i:2 * i + 2, 2:2 + S], turned_)
                elif i == 4:
                    last = V.tensor_copy(vo[:, :, 0:256], tokens_)
                elif i < 10:
                    last = V.tensor_copy(dqk[:, 2 * (i - 6):2 * (i - 6) + 2, :], turned_)
                elif i == 10:
                    last = V.tensor_copy(dv[:, :, 0:256], tokens_)
                else:
                    last = V.tensor_copy(vo[:, :, MW:MW + 256], tokens_)
                last.then_inc(mix_out[0], 1)
                if i == 2:
                    gate_rows_program()
                if i in (4, 6):
                    dve.wait_ge(mix_out[0], 2)
                    dve.wait_ge(mix_out[1], 2)
                    for c in range(4 * (i // 2 - 2), 4 * (i // 2 - 1)):
                        convolve(c)
                if i == 8:
                    dve.wait_ge(gate_cols, 1)
                    V.tensor_copy(rowcols[:, :, :, :], PS[:, 5, 0:216].rearrange("p (n t m) -> p n t m", n=3, t=NT))\
                        .then_inc(gate_cols_set, 1)
                    dve.wait_ge(late_in, 16 * 7)
                    then(V.tensor_tensor(lambc[:, 0, :], lambc[:, 0, :], lambc[:, 1, :], ALU.mult))
                    then(V.tensor_tensor(lambc[:, 2, :], lambc[:, 2, :], lambc[:, 3, :], ALU.mult))
                    V.tensor_reduce(lam[:, 0:1], lambc[:, 0, :], AX_X, ALU.add)
                    V.tensor_reduce(lam[:, 1:2], lambc[:, 2, :], AX_X, ALU.add).then_inc(lam_dots, 1)
                    dve.wait_ge(lam_exps, 1)
                    then(V.tensor_tensor(lam[:, 4:5], lam[:, 3:4], lam[:, 2:3], ALU.subtract))
                    V.tensor_scalar(lam[:, 5:6], lam[:, 4:5], -LAM_INIT, None, ALU.add).then_inc(lam_set, 1)

            def mlstm_args(u):
                b, E = 2 * (u % 2), expo[:, u % 2, :]
                M = lambda d, t: rowcols[:, 1, t, 32 * d + u:32 * d + u + 1]
                f, w = PS[:, b + 1, 0:S], PS[:, b + 1, S:2 * S]
                V.scalar_tensor_tensor(E[:, 0:256], f, M(0, 1), keepf, ALU.subtract, ALU.min)
                V.scalar_tensor_tensor(E[:, 256:512], w, M(1, 0), keepb, ALU.subtract, ALU.min)
                V.scalar_tensor_tensor(E[:, 512:640], f[:, 0:P], M(0, 0), keepf[:, P:S], ALU.subtract, ALU.min)
                V.scalar_tensor_tensor(E[:, 640:768], w[:, P:S], M(1, 1), keepb[:, 0:P], ALU.subtract, ALU.min)\
                    .then_inc(unit_arg, 1)

            def mlstm_combine(u):
                b, E, s = 2 * (u % 2), expo[:, u % 2, :], unit_s[:, u, :]
                dve.wait_ge(unit_exp, u + 1)
                for n, (o, c, z) in enumerate([(0, 256, 256), (256, 0, 256), (512, 0, 128), (640, 384, 128)]):
                    last = V.scalar_tensor_tensor(E[:, o:o + z], PS[:, b, c:c + z], P ** -0.5, E[:, o:o + z], ALU.mult,
                                                  ALU.mult, accum_out=s[:, n:n + 1])
                last.then_inc(unit_read, 1)
                dve.wait_ge(unit_read, u + 1)
                then(V.scalar_tensor_tensor(s[:, 12:16], s[:, 0:4], -1.0, s[:, 0:4], ALU.mult, ALU.max))
                for n, (d, t) in enumerate([(0, 1), (1, 0), (0, 0), (1, 1)]):
                    last = V.tensor_tensor(s[:, 4 + n:5 + n], s[:, 12 + n:13 + n],
                                           rowcols[:, 2, t, 32 * d + u:32 * d + u + 1], ALU.max)
                then(last)
                then(V.reciprocal(s[:, 8:12], s[:, 4:8]))
                if u >= 1:
                    dve.wait_ge(unit_turned, u)
                then(V.tensor_scalar(comb[:, 1, :], E[:, 0:256], s[:, 8:9], None, ALU.mult))
                then(V.tensor_scalar(comb[:, 0, :], E[:, 256:512], s[:, 9:10], None, ALU.mult))
                V.scalar_tensor_tensor(comb[:, 0, 0:P], E[:, 512:640], s[:, 10:11], comb[:, 0, 0:P], ALU.mult, ALU.add)
                V.scalar_tensor_tensor(comb[:, 1, P:S], E[:, 640:768], s[:, 11:12], comb[:, 1, P:S], ALU.mult, ALU.add)\
                    .then_inc(unit_comb, 1)

            def diff_args(u):
                b, E, s = 2 * (u % 2), expo[:, u % 2, :], unit_s[:, u, :]
                dve.wait_ge(alibi_set, u - MH + 1)
                for t in range(NT):
                    Et = E[:, 512 * t:512 * (t + 1)].rearrange("p (c s) -> p c s", c=2)
                    last = V.scalar_tensor_tensor(Et, PS[:, b:b + 2, t * S:(t + 1) * S], HD ** -0.5,
                                                  alibi[:, t:t + 1, :].to_broadcast([P, 2, S]), ALU.mult, ALU.add)
                last.then_inc(unit_read, 1)
                dve.wait_ge(unit_read, u + 1)
                V.tensor_reduce(s[:, 0:4], E.rearrange("p (c s) -> p c s", c=4), AX_X, ALU.max, negate=True)\
                    .then_inc(unit_arg, 1)

            def diff_combine(u):
                E, s = expo[:, u % 2, :], unit_s[:, u, :]
                dve.wait_ge(unit_exp, u + 1)
                then(V.reciprocal(s[:, 8:12], s[:, 4:8]))
                for t in range(NT):
                    last = V.tensor_scalar(s[:, 12 + t:13 + t], s[:, 9 + 2 * t:10 + 2 * t], lam[:, 5:6], None, ALU.mult)
                then(last)
                dve.wait_ge(unit_turned, u)
                for t in range(NT):
                    then(V.tensor_scalar(comb[:, t, :], E[:, 512 * t:512 * t + S], s[:, 8 + 2 * t:9 + 2 * t], None,
                                         ALU.mult))
                    last = V.scalar_tensor_tensor(comb[:, t, :], E[:, 512 * t + S:512 * (t + 1)], s[:, 12 + t:13 + t],
                                                  comb[:, t, :], ALU.mult, ALU.add)
                last.then_inc(unit_comb, 1)

            def unit_args(u):
                dve.wait_ge(unit_scored, u + 1)
                if u >= 2:
                    dve.wait_ge(unit_comb, u - 1)
                (mlstm_args if u < MH else diff_args)(u)

            dve.wait_ge(lam_set, 1)
            unit_args(0)
            for u in range(2 * MH):
                if u < MH:
                    mlstm_combine(u)
                else:
                    diff_combine(u)
                if u + 1 < 2 * MH:
                    unit_args(u + 1)
                dve.wait_ge(unit_out, u + 1)
                V.tensor_copy(work[:, :, u * P:(u + 1) * P], PS[:, 5, 0:S].rearrange("p (t n) -> p t n", t=NT))\
                    .then_inc(raw_set, 1)
            dve.wait_ge(raw_set, 8)

            for t in range(NT):
                for u in range(8):
                    last = V.bn_stats(bn6[:, 8 * t + u, :], work[:, t, u * P:(u + 1) * P])
            then(last)
            for n in range(16):
                last = V.bn_aggr(mv[:, n, :], bn6[:, n, :])
            then(last)
            var = bn6[:, :, 0]
            mvt = mv.rearrange("p (t u) c -> p t u c", t=NT)
            b6t = bn6.rearrange("p (t u) c -> p t u c", t=NT)
            then(V.tensor_tensor(b6t[:, :, 4:8, 1], mvt[:, :, 4:8, 0], mvt[:, :, 4:8, 0], ALU.mult))
            then(V.tensor_tensor(mvt[:, :, 4:8, 1], mvt[:, :, 4:8, 1], b6t[:, :, 4:8, 1], ALU.add))
            V.tensor_scalar(var, mv[:, :, 1], EPS, None, ALU.add).then_inc(var2_set, 1)
            dve.wait_ge(root2_set, 1)
            then(V.reciprocal(bn6[:, :, 3], bn6[:, :, 2]))
            dve.wait_ge(osig_set, 1)
            for t in range(NT):
                for u in range(8):
                    n = 8 * t + u
                    w = work[:, t, u * P:(u + 1) * P]
                    if u < MH:
                        last = V.tensor_scalar(w, w, mv[:, n, 0:1], bn6[:, n, 3:4], ALU.subtract, ALU.mult)
                    else:
                        last = V.tensor_scalar(w, w, bn6[:, n, 3:4], 1.0 - LAM_INIT, ALU.mult, ALU.mult)
                then(last)
                V.tensor_tensor(work[:, t, 0:MW], work[:, t, 0:MW], vo[:, t, MW:2 * MW], ALU.mult).then_inc(normed, 1)
            mixT = mixin[:, :, :].rearrange("p t d -> p (t d)").rearrange("p (k s) -> p k s", k=KD)
            place(TBRANCH, 0, mixT,
                  lambda k: colB[:, B_MLN + k:B_MLN + k + 1] if k < MH else colB[:, B_DNG:B_DNG + 1], None)
            hflat = hT[:, :, :].rearrange("p k s -> p (k s)")
            for half in range(2):
                for br in range(2):
                    dve.wait_ge(slots_used, used(G_UP + 2 * half + br))
                    dve.wait_ge(gsig_set, 2 * half + br + 1)
                    ps = PS[:, 4 * half + 2 * br:4 * half + 2 * br + 2, :].rearrange("p b n -> p (b n)")
                    gate = gT[:, 8 * br + 4 * half:8 * br + 4 * half + 4, :].rearrange("p k s -> p (k s)")
                    dst = (hflat[:, 1024 * half:1024 * (half + 1)], work[:, half, :])[br]
                    last = V.tensor_tensor(dst, ps, gate, ALU.mult)
                then(last)
                V.tensor_tensor(hflat[:, 1024 * half:1024 * (half + 1)], hflat[:, 1024 * half:1024 * (half + 1)],
                                work[:, half, :], ALU.add).then_inc(mixed, 1)
            for i in range(N_WOUT2):
                dve.wait_ge(slots_used, used(G_WOUT2 + i))
                xs = xres[:, :, 256 * i:256 * (i + 1)]
                V.tensor_tensor(xs, xs, PS[:, i, :].rearrange("p (t n) -> p t n", t=NT), ALU.add).then_inc(x3_set, 1)
            dve.wait_ge(x3_set, 4)

            norm(N4)
            place(T4, 4, hT, lambda k: colB[:, B_NFFN + k:B_NFFN + k + 1], None)
            dve.wait_ge(logit16, 1)
            V.tensor_reduce(aff_s[:, 0:2], PS[:, 0, 0:32].rearrange("p (t e) -> p t e", t=NT), AX_X, ALU.max, negate=True)\
                .then_inc(negmax16, 1)
            dve.wait_ge(exp16, 1)
            then(V.reciprocal(aff_s[:, 4:6], aff_s[:, 2:4]))
            for t in range(NT):
                last = V.tensor_scalar(aff[:, t, :], aff[:, t, :], aff_s[:, 4 + t:5 + t], None, ALU.mult)
            last.then_inc(aff_set, 1)
            dve.wait_ge(aff_set, 1)

            def compare(q):
                dve.wait_ge(affbc_set, q + 1)
                if q >= 2:
                    dve.wait_ge(rank_cols, 2 * (q - 1))
                E = slice(4 * (q % 2), 4 * (q % 2) + 4)
                other = affbc[:, 4 * q:4 * q + 4, :]
                own = lambda i, n: aff[:, i, 4 * q:4 * q + 4].unsqueeze(2).to_broadcast([P, 4, n])
                V.tensor_tensor(beats[:, 0, E, 0:P], other[:, :, 0:P], own(0, P), ALU.is_lt)
                V.tensor_tensor(beats[:, 0, E, P:S], other[:, :, P:S], own(0, P), ALU.is_le)
                V.tensor_tensor(beats[:, 1, E, :], other, own(1, S), ALU.is_lt)
                for i in range(NT):
                    last = V.tensor_tensor(beats_eq[:, i, E, :], other[:, :, i * P:(i + 1) * P], own(i, P), ALU.is_equal)
                then(last)
                for i in range(NT):
                    last = V.tensor_tensor(beats_eq[:, i, E, :], beats_eq[:, i, E, :],
                                           tie.unsqueeze(1).to_broadcast([P, 4, P]), ALU.mult)
                last.then_inc(beats_set, 1)

            def choose(q):
                dve.wait_ge(rank_spread, q + 1)
                V.scalar_tensor_tensor(selTg[:, 2 * q:2 * q + 2, :].rearrange("p e t -> p (e t)"), PS[:, 4 + q % 2, :],
                                       slotcol, affbc[:, 2 * q:2 * q + 2, :].rearrange("p e t -> p (e t)"), ALU.is_equal,
                                       ALU.mult).then_inc(selT_set, 1)

            compare(0)
            for q in range(4):
                if q + 1 < 4:
                    compare(q + 1)
                choose(2 * q)
                choose(2 * q + 1)
            dve.wait_ge(rank_cols, 8)
            V.tensor_copy(rankc[:, :, :], PS[:, 6, 0:32].rearrange("p (t e) -> p t e", t=NT)).then_inc(rankc_set, 1)
            dve.wait_ge(rankc_set, 1)
            for t in range(NT):
                V.tensor_tensor(sel[:, t, :].rearrange("p (e c) -> p e c", e=EXPERTS),
                                slotrow.unsqueeze(1).to_broadcast([P, EXPERTS, CAP]),
                                rankc[:, t, :].unsqueeze(2).to_broadcast([P, EXPERTS, CAP]), ALU.is_equal)\
                    .then_inc(sel_set, 1)
            for k in range(KD):
                dve.wait_ge(gathered, k + 1)
                V.tensor_scalar(xeT[:, k, :], PS[:, k % 4, :], colB[:, B_NFFN + k:B_NFFN + k + 1], None, ALU.mult)\
                    .then_inc(xe_out, 1)

            with dve.Fori(0, EXPERTS) as e:
                dve.wait_ge(slots_used, e * PER_EXPERT + used(G_EXPERTS + 15))
                dve.wait_ge(silu_set, e + 1)
                V.tensor_tensor(hid[:, :], silu[:, :], PS[:, 1, :], ALU.mult).then_inc(hid_set, 1)
                dve.wait_ge(hid_turned, e + 1)
                V.tensor_copy(hidT[:, :, :, :].rearrange("p c j t -> p (c j t)"), PS[:, 2, :]).then_inc(hidT_set, 1)

            dve.wait_ge(scattered, EXPERTS + 1)
            for t in range(NT):
                V.tensor_copy(xres[:, t, :], PS[:, 4 + 2 * t:6 + 2 * t, :].rearrange("p b n -> p (b n)"))\
                    .then_inc(final_copied, 1)
            variance(NLAST)
            dve.wait_ge(gfinal_in, 16)
            for t in range(NT):
                V.scalar_tensor_tensor(work[:, t, :], xres[:, t, :], stats[:, NLAST, 6 + t:7 + t], gfinal, ALU.mult,
                                       ALU.mult).then_inc(final_set, 1)

        @block.scalar
        def _(act):
            N = nc.scalar
            then = Chain(act, act_chain)
            a0 = lambda ap: ap[0]

            act.dma_start(const[:, :], A["shape_constants"]).then_inc(consts_in, 16)
            act.dma_start(rowsA[A_GAIN:A_GAIN + 32, :], A["norm_gains"][0].rearrange("g (c p) -> (g c) p", p=P))\
                .then_inc(rows_in, 16)
            for at, n, name in ((A_BADA, 48, "b_ada"), (A_B1, 32, "b1")):
                act.dma_start(rowsA[at:at + n, :], A[name][0].rearrange("(c p) -> c p", p=P)).then_inc(rows_in, 16)
            act.dma_start(rowsB[B_CONVW:B_CONVW + 40, :], A["conv_w_2"][0].rearrange("j (c p) -> (j c) p", p=P))\
                .then_inc(rows_in, 16)
            for at, n, name in ((B_CONVB, 8, "conv_b_2"), (B_NMIX, 8, "norm_mix_g_2"), (B_NFFN, 8, "norm_ffn_g_2"),
                                (B_MLN, 4, "mlstm_norm_g_2"), (B_DNG, 1, "diff_norm_g_2"), (B_C, 8, "c")):
                act.dma_start(rowsB[at:at + n, :], A[name][0].rearrange("(c p) -> c p", p=P)).then_inc(rows_in, 16)
            act.dma_start(xres[:, :, :], A["x"][0].rearrange("(t p) d -> p t d", p=P)).then_inc(x_in, 16)

            def everywhere(row, n):
                return bass.AP(row.tensor, row.offset, [[0, P], [1, n]])

            act.dma_start(relb[:, :], A["rel_bias"]).then_inc(late_in, 16)
            act.dma_start(sinkbc[:, :], everywhere(A["sinks"], 8)).then_inc(late_in, 16)
            act.dma_start(lambc[:, :, :].rearrange("p a d -> p (a d)"), everywhere(A["diff_lam_2"], 256)).then_inc(late_in, 16)
            act.dma_start(router[:, :, :], A["w_router_2"][0].rearrange("(k p) e -> p k e", p=P)).then_inc(late_in, 16)
            act.dma_start(mgate[:, :, :], w_in2[:, :, GATE0:GATE0 + 16]).then_inc(mg_in, 16)
            act.wait_ge(bmg_set, 1)
            for part, col, at in ((0, 0, 0), (0, 1, 4), (32, 0, 8), (32, 1, 12)):
                act.dma_start(bmg[part:part + 4, col:col + 1], A["b_mgate_2"][0, at:at + 4].rearrange("(a b) -> a b", b=1))\
                    .then_inc(mg_in, 16)
            act.dma_start(b2bc, everywhere(A["b2"], D)).then_inc(late_in, 16)
            act.dma_start(G1, everywhere(A["norm_gains"][0, 1], D)).then_inc(late_in, 16)
            act.dma_start(G2, everywhere(A["norm_gains"][0, 3], D)).then_inc(late_in, 16)

            def squares(n, src, junk):
                for t in range(NT):
                    N.activation(junk[:, t, :], src[:, t, :], ACT.Square, accum_out=stats[:, n, t:t + 1])\
                        .then_inc(squared, 1)
                act.wait_ge(variance_set, n + 1)
                N.activation(stats[:, n, 4:6], stats[:, n, 2:4], ACT.Sqrt).then_inc(root_set, 1)

            def place(n, base, dst, scale, shift):
                for j in (1, 3):
                    act.wait_ge(turned, 4 * n + j + 1)
                    for q in range(4):
                        k = 4 * (j % 2) + q
                        o, i = dst[:, k, (j // 2) * P:(j // 2 + 1) * P], PS[:, base + j, q * P:(q + 1) * P]
                        last = N.activation(o, i, ACT.Identity, scale=scale(k), bias=(0.0 if shift is None else shift(k)))
                    last.then_inc(placed, 1)

            act.wait_ge(cols_set, 1)
            N.activation(cact[:, :], colB[:, B_C:B_C + KD], ACT.Silu).then_inc(c_acted, 1)
            act.wait_ge(x_in, 16)
            squares(N1, xres, work)
            act.wait_ge(bias_row_set, 1)
            act.dma_start(bias_scratch, logits[0:HEADS, 0, :]).then_inc(bias_stored, 16)
            act.wait_ge(bias_stored, 16)
            for h in range(HEADS):
                src = bass.AP(bias_scratch.tensor, bias_scratch.offset + h * 384, [[1, P], [1, S]])
                act.dma_start(biasm[:, h, 0:S], src).then_inc(bias_in, 16)
            act.wait_ge(folded, 1)
            shift1 = modcol[:, 0, 0:2, :].rearrange("p j q -> p (j q)")
            place(T1, 4, hT, lambda k: fold[:, 0, k:k + 1], lambda k: shift1[:, k:k + 1])
            for i in range(1, N_WIN, 2):
                act.wait_ge(slots_used, used(G_WIN + i))
                if i == 5:
                    N.activation(v1[:, :, 256:512], PS[:, i % 4, :].rearrange("p (t n) -> p t n", t=NT), ACT.Copy)\
                        .then_inc(win_out[1], 1)
                else:
                    chunk = {1: 2, 3: 6, 7: 10}[i]
                    N.activation(qk_chunks(chunk), PS[:, i % 4, :].rearrange("p (m s) -> p m s", m=4), ACT.Copy)\
                        .then_inc(win_out[1], 1)
            act.wait_ge(win_out[0], 5)
            for a, b in ((0, 64), (64, 0)):
                act.dma_start(qkT[a:a + 64, 13, :], qkT[b:b + 64, 12, :]).then_inc(kswap_in, 16)
            bg = A["b_ada"][0]
            act.dma_start(ybuf[:, 0, :], everywhere(bg[2 * D:3 * D], D)).then_inc(bg_in, 16)
            act.dma_start(ybuf[:, 1, :], everywhere(bg[5 * D:6 * D], D)).then_inc(bg_in, 16)

            for h in range(HEADS + 2):
                if h < HEADS:
                    s, L, Pr = att_s[:, h, :], logits[:, h % 2, :], probs[:, h % 2, :]
                    act.wait_ge(negmax_set, h + 1)
                    if h >= 2:
                        act.wait_ge(probs_turned, h - 1)
                    N.activation(Pr[:, 0:S], L[:, 0:S], ACT.Exp, bias=s[:, 0:1], accum_out=s[:, 2:3])
                    last = N.activation(Pr[:, S:384], L[:, S:384], ACT.Exp, bias=s[:, 1:2], accum_out=s[:, 3:4])
                    if h >= 8:
                        last = N.activation(s[:, 4:6], s[:, 0:2], ACT.Exp, bias=sinkbc[:, h - 8:h - 7])
                    last.then_inc(exp_set, 1)
                if 1 <= h <= HEADS:
                    g = h - 1
                    act.wait_ge(probs_turned, g + 1)
                    if g >= 2:
                        act.wait_ge(weighed, g - 1)
                    N.activation(probsT[:, g % 2, :].rearrange("p (b s) -> p b s", b=3)[:, :, ::-1],
                                 PS[:, 2 + g % 2, 0:384].rearrange("p (b s) -> p b s", b=3), ACT.Copy)\
                        .then_inc(probsT_set, 1)
                if h >= 2 and h % 2 == 1:
                    pair = (h - 2) // 2
                    act.wait_ge(weighed, 2 * pair + 2)
                    N.activation(attT[:, pair, :], PS[:, 4 + pair % 2, 0:S], ACT.Copy).then_inc(att_out, 1)
            for i in (1, 3):
                act.wait_ge(slots_used, used(G_WOUT + i))
                N.activation(ybuf[:, :, 256 * i:256 * (i + 1)], PS[:, i, :].rearrange("p (t n) -> p t n", t=NT), ACT.Copy)\
                    .then_inc(wout_out[1], 1)
            act.wait_ge(wout_out[0], 2)
            act.wait_ge(wout_out[1], 2)
            squares(POST1, ybuf, work)
            act.wait_ge(x1_set, 2)
            squares(N2, xres, work)
            shift2 = modcol[:, 1, 2:4, :].rearrange("p j q -> p (j q)")
            place(T2, 4, hT, lambda k: fold[:, 1, k:k + 1], lambda k: shift2[:, k:k + 1])
            for i in range(N_W1):
                act.wait_ge(w1_relu, 2 * i + 2)
                N.activation(ffT[:, 2 * i:2 * i + 2, :].rearrange("p m s -> p (m s)"), relu[:, i % 2, :], ACT.Square)\
                    .then_inc(w1_out, 1)
            act.wait_ge(w2_out, 2)
            squares(POST2, ybuf, work)
            act.wait_ge(x2_set, 2)
            squares(N3, xres, work)
            place(T3, 0, hT, lambda k: colB[:, B_NMIX + k:B_NMIX + k + 1], None)

            for i in range(1, N_MIX2, 2):
                act.wait_ge(slots_used, used(G_MIX2 + i))
                turned_ = PS[:, i % 4, :].rearrange("p (m s) -> p m s", m=2)
                tokens_ = PS[:, i % 4, :].rearrange("p (t n) -> p t n", t=NT)
                if i == 1:
                    act.wait_ge(pads_set, 2)
                if i < 4:
                    dst, src = zpad[:, 2 * i:2 * i + 2, 2:2 + S], turned_
                elif i == 5:
                    dst, src = vo[:, :, 256:512], tokens_
                elif i < 10:
                    dst, src = dqk[:, 2 * (i - 6):2 * (i - 6) + 2, :], turned_
                elif i == 11:
                    dst, src = dv[:, :, 256:512], tokens_
                else:
                    dst, src = vo[:, :, MW + 256:2 * MW], tokens_
                N.activation(dst, src, ACT.Copy).then_inc(mix_out[1], 1)
                if i == 3:
                    R = rows2[0:36, :, :]
                    act.wait_ge(gate_rows_set, 1)
                    then(N.activation(R[:, 2, :], R[:, 2, :], ACT.Exp))
                    N.activation(R[:, 2, :], R[:, 2, :], ACT.Ln, bias=1.0).then_inc(gate_ln, 1)
                    act.wait_ge(gate_m, 2)
                    N.activation(R[:, 7, :], R[:, 7, :], ACT.Exp, scale=-1.0).then_inc(gate_em, 1)
                if i in (5, 7):
                    for c in range(4 * (i // 2 - 2), 4 * (i // 2 - 1)):
                        act.wait_ge(conv_set, c + 1)
                        N.activation(qkc[:, c, :], conv[:, c % 2, :], ACT.Silu).then_inc(qk_set, 1)
                if i == 9:
                    act.wait_ge(lam_dots, 1)
                    N.activation(lam[:, 2:4], lam[:, 0:2], ACT.Exp).then_inc(lam_exps, 1)

            for u in range(2 * MH):
                E, s = expo[:, u % 2, :], unit_s[:, u, :]
                act.wait_ge(unit_arg, u + 1)
                if u < MH:
                    N.activation(E[:, 0:768], E[:, 0:768], ACT.Exp).then_inc(unit_exp, 1)
                else:
                    for n in range(4):
                        last = N.activation(E[:, n * S:(n + 1) * S], E[:, n * S:(n + 1) * S], ACT.Exp,
                                            bias=s[:, n:n + 1], accum_out=s[:, 4 + n:5 + n])
                    last.then_inc(unit_exp, 1)
                act.wait_ge(slots_used, used(G_GATES2 + u))
                N.activation(gT[:, 2 * u:2 * u + 2, :].rearrange("p m s -> p (m s)"), PS[:, 6 + u % 2, :], ACT.Copy)\
                    .then_inc(gates_out, 1)
                act.wait_ge(unit_turned, u + 1)
                if u >= 1:
                    act.wait_ge(unit_out, u)
                N.activation(combT[:, :, :].rearrange("p j s -> p (j s)"), PS[:, 4, :], ACT.Copy).then_inc(unit_T, 1)
            act.wait_ge(mix_out[0], N_MIX2 // 2)
            N.activation(vo[:, :, MW:2 * MW], vo[:, :, MW:2 * MW], ACT.Sigmoid).then_inc(osig_set, 1)
            act.wait_ge(var2_set, 1)
            N.activation(bn6[:, :, 2], bn6[:, :, 0], ACT.Sqrt).then_inc(root2_set, 1)
            mixT = mixin[:, :, :].rearrange("p t d -> p (t d)").rearrange("p (k s) -> p k s", k=KD)
            place(TBRANCH, 0, mixT,
                  lambda k: colB[:, B_MLN + k:B_MLN + k + 1] if k < MH else colB[:, B_DNG:B_DNG + 1], None)
            act.wait_ge(gates_out, 8)
            for half in range(2):
                for br in range(2):
                    g = gT[:, 8 * br + 4 * half:8 * br + 4 * half + 4, :].rearrange("p k s -> p (k s)")
                    N.activation(g, g, ACT.Sigmoid).then_inc(gsig_set, 1)
            act.wait_ge(x3_set, 4)
            squares(N4, xres, ybuf)
            place(T4, 4, hT, lambda k: colB[:, B_NFFN + k:B_NFFN + k + 1], None)
            act.wait_ge(negmax16, 1)
            for t in range(NT):
                last = N.activation(aff[:, t, :], PS[:, 0, t * EXPERTS:(t + 1) * EXPERTS], ACT.Exp,
                                    bias=aff_s[:, t:t + 1], accum_out=aff_s[:, 2 + t:3 + t])
            last.then_inc(exp16, 1)
            for q in range(4):
                act.wait_ge(aff_spread, q + 1)
                b = 2 * (q % 2)
                N.activation(affbc[:, 4 * q:4 * q + 4, :].rearrange("p e t -> p (e t)"),
                             PS[:, b:b + 2, :].rearrange("p b n -> p (b n)"), ACT.Copy).then_inc(affbc_set, 1)
            act.dma_start(gfinal, everywhere(A["norm_f_g_2"], D)).then_inc(gfinal_in, 16)
            act.wait_ge(selT_set, 8)
            with act.Fori(0, EXPERTS) as e:
                act.wait_ge(slots_used, e * PER_EXPERT + used(G_EXPERTS + 7))
                N.activation(silu[:, :], PS[:, 0, :], ACT.Silu).then_inc(silu_set, 1)
                act.wait_ge(slots_used, e * PER_EXPERT + used(G_EXPERTS + 23))
                N.activation(ye[:, :], PS[:, 3, :], ACT.Copy).then_inc(ye_set, 1)
            for t in range(NT):
                act.wait_ge(final_copied, t + 1)
                N.activation(work[:, t, :], xres[:, t, :], ACT.Square, accum_out=stats[:, NLAST, t:t + 1])\
                    .then_inc(squared, 1)
            act.wait_ge(variance_set, NLAST + 1)
            N.activation(stats[:, NLAST, 4:6], stats[:, NLAST, 2:4], ACT.Sqrt).then_inc(root_set, 1)

        @block.gpsimd
        def _(pool):
            G = nc.gpsimd
            then = Chain(pool, pool_chain)
            pool.wait_ge(bias_in, 16 * HEADS)
            G.tensor_copy(biasm[:, :, S:384], biasm[:, :, P:S]).then_inc(bias_copied, 1)
            pool.wait_ge(x2_set, 2)
            G.memset(zpad[:, :, 0:2], 0.0)
            G.memset(zpad[:, :, S + 2:S + 4], 0.0).then_inc(pads_set, 1)
            G.memset(rows2[0:36, :, :], 0.0).then_inc(pads_set, 1)
            pool.wait_ge(mg_in, 16 * 5)
            G.memset(wgi, 0.0)
            then(G.memset(wgf, 0.0))
            for w, at in ((wgi, 0), (wgf, 4)):
                for d in range(2):
                    G.tensor_copy(w[:, :, 32 * d:32 * d + 4], mgate[:, :, at + 8 * d:at + 8 * d + 4]).then_inc(wg_set, 1)
            for h in range(MH):
                if h >= 1:
                    pool.wait_ge(unit_read, MH + h)
                slope = 2.0 ** (-8.0 * (h + 1) / MH)
                G.tensor_scalar(alibi[:, :, :].rearrange("p t s -> p (t s)"), dist, -slope, None, ALU.mult)\
                    .then_inc(alibi_set, 1)
            pool.wait_ge(xe_out, KD)
            pool.wait_ge(selT_set, 8)
            with pool.Fori(0, EXPERTS) as e:
                pool.wait_ge(slots_used, e * PER_EXPERT + used(G_EXPERTS + 15 - PER_EXPERT))
                G.tensor_copy(xe[:, :, :], xeT[:, :, bass.ds(e * CAP, CAP)]).then_inc(xe_ready, 1)
                pool.wait_ge(scattered, e + 1)
                G.tensor_copy(selx[:, :], selTg[:, bass.ds(e, 1), :].rearrange("p o t -> p (o t)"))\
                    .then_inc(selx_ready, 1)


_INS = ["x", "c", "w_in", "w_out", "sinks", "rel_bias", "w_ada", "b_ada", "norm_gains", "w1", "b1", "w2", "b2",
        "norm_mix_g_2", "w_in_2", "b_mgate_2", "conv_w_2", "conv_b_2", "mlstm_norm_g_2", "diff_lam_2", "diff_norm_g_2",
        "w_up_a_2", "w_up_b_2", "w_out_2", "norm_ffn_g_2", "w_router_2", "w_gate_e_2", "w_up_e_2", "w_down_e_2",
        "norm_f_g_2"]


def kernel(**inputs):
    import concourse.bacc as _bacc
    from concourse.bass_utils import run_bass_kernel_spmd as _run

    nc = _bacc.Bacc("TRN2", target_bir_lowering=False, num_devices=1)
    arrays, aps = {}, {}
    for name in _INS + ["shape_constants"]:
        a = shape_constants() if name == "shape_constants" else np.ascontiguousarray(inputs[name])
        if name == "norm_f_g_2":
            a = a.reshape(1, D)
        arrays[f"in_{name}"] = a
        aps[name] = nc.dram_tensor(f"in_{name}", a.shape, mybir.dt.from_np(a.dtype), kind="ExternalInput").ap()
    out = nc.dram_tensor("out", (1, S, D), F32, kind="ExternalOutput").ap()
    bias_scratch = nc.dram_tensor("bias_scratch", [HEADS, 384], F32, kind="Internal").ap()
    build_program(nc, aps, out, bias_scratch)
    r = _run(nc, [arrays], core_ids=[0])
    return r.results[0]["out"]
```

```python
from contextlib import ExitStack
import math

import numpy as np

import concourse.bass as bass
from concourse import mybir

ALU = mybir.AluOpType
ACT = mybir.ActivationFunctionType
AX_X = mybir.AxisListType.X
F32 = mybir.dt.float32
BF16 = mybir.dt.bfloat16
F32R = mybir.dt.float32r

P = 128
S = 256
D = 1024
NT = S // P
KD = D // P
HD = 64
HEADS = 16
BUCKETS = 32
W_A = 512
D_FF = 4096
MH = 4
MW = 512
EXPERTS = 16
CAP = 32
D_EXP = 2048
EPS = 1e-6
BIG = 3e38
MASKED = -1e30
LAM_INIT = 0.8 - 0.6 * math.exp(-0.3 * 0)
GATE0 = 2048
DIFF0 = GATE0 + 16

SLOT = 2048
RING = 12
N_ADA0, N_WIN, N_ADA12, N_WOUT, N_W1, N_W2, N_MIX2, N_GATES2, N_UP, N_WOUT2 = 8, 9, 16, 4, 16, 16, 14, 8, 4, 4
PRELUDE = N_ADA0 + N_WIN + N_ADA12 + N_WOUT + N_W1 + N_W2 + N_MIX2 + N_GATES2 + N_UP + N_WOUT2
PER_EXPERT = 24
assert PER_EXPERT % RING == 0
RING_P = 6
MLP_HALF = N_W1 // 2
G_ADA0 = 0
G_WIN = G_ADA0 + N_ADA0
G_ADA12 = G_WIN + N_WIN
G_WOUT = G_ADA12 + N_ADA12
G_MLP = G_WOUT + N_WOUT
G_MIX2 = G_MLP + N_W1 + N_W2
G_GATES2 = G_MIX2 + N_MIX2
G_UP = G_GATES2 + N_GATES2
G_WOUT2 = G_UP + N_UP
G_EXPERTS = G_WOUT2 + N_WOUT2
assert G_EXPERTS == PRELUDE
SPLIT = [g for g in range(PRELUDE) if g >= G_WIN and not G_ADA12 <= g < G_WOUT]
BY_POOL = [g for g in SPLIT if G_MIX2 <= g < G_UP]
BY_DVE = [g for g in SPLIT if g not in BY_POOL]


def g_w1(i):
    return G_MLP + 2 * MLP_HALF * (i // MLP_HALF) + i % MLP_HALF


def g_w2(i):
    return g_w1(i) + MLP_HALF


C_IDENT = 0
C_SLOTCOL = C_IDENT + P
C_SLOTROW = C_SLOTCOL + 1
C_TIE = C_SLOTROW + CAP
C_KEEPF = C_TIE + P
C_KEEPB = C_KEEPF + S
C_DIST = C_KEEPB + S
C_ONEHOT = C_DIST + NT * S
C_MASK = C_ONEHOT + 384
C_END = C_MASK + 384

A_GAIN, A_BADA, A_B1, A_ROWS = 0, 32, 80, 112
B_CONVW, B_CONVB, B_NMIX, B_NFFN, B_MLN, B_DNG, B_C, B_ROWS = 0, 40, 48, 56, 64, 68, 69, 77


def shape_constants():
    c = np.zeros((P, C_END), np.float32)
    p = np.arange(P)
    c[:, C_IDENT:C_IDENT + P] = np.eye(P)
    c[:, C_SLOTCOL] = p % CAP
    c[:, C_SLOTROW:C_SLOTROW + CAP] = np.arange(CAP)
    c[:, C_TIE:C_TIE + P] = p[:, None] < p[None, :]
    lower = np.where(p[None, :] <= p[:, None], BIG, -BIG)
    c[:, C_KEEPF:C_KEEPF + P] = BIG
    c[:, C_KEEPF + P:C_KEEPF + S] = lower
    c[:, C_KEEPB:C_KEEPB + P] = lower.T
    c[:, C_KEEPB + P:C_KEEPB + S] = BIG
    for t in range(NT):
        c[:, C_DIST + t * S:C_DIST + (t + 1) * S] = np.abs(t * P + p[:, None] - np.arange(S)[None, :])
    dist = S - 1 - np.arange(383)
    n = np.maximum(dist, 0)
    half = BUCKETS // 2
    large = half + (np.log(np.maximum(n, 1).astype(np.float32) / half) / math.log(128 / half) * half).astype(np.int32)
    bucket = np.where(n < half, n, np.minimum(large, BUCKETS - 1))
    c[bucket, C_ONEHOT + np.arange(383)] = 1.0
    c[:8, C_MASK:C_MASK + 383] = np.where(dist < 0, MASKED, 0.0)
    c[8:16, C_MASK:C_MASK + 383] = np.where((dist < 0) | (dist >= 128), MASKED, 0.0)
    return c


def build_program(nc, A, out, bias_scratch):
    with ExitStack() as ctx:
        def sb(name, shape, dt=F32):
            return ctx.enter_context(nc.sbuf_tensor(name, shape, dt))

        def sems(text):
            return [ctx.enter_context(nc.semaphore(n)) for n in text.split()]

        ring = sb("ring", [P, RING, SLOT])
        ring_at = nc.sbuf_base - 4 * RING * SLOT
        ARENA = 16896
        arena = sb("arena", [P, ARENA])
        arena_at = nc.sbuf_base - 4 * ARENA
        wR = nc.alloc_sbuf_tensor_at("wR", [P, 2, 2, SLOT], F32R, offset=ring_at + 4 * RING_P * SLOT)
        hR = nc.alloc_sbuf_tensor_at("hR", [P, 2, KD, S], F32R, offset=ring_at + 4 * (RING_P + 4) * SLOT)
        fR = nc.alloc_sbuf_tensor_at("fR", [P, 2, 2 * MLP_HALF, S], F32R, offset=arena_at)
        const = sb("const", [P, C_END])
        ident = const[:, C_IDENT:C_IDENT + P]
        slotcol = const[:, C_SLOTCOL:C_SLOTCOL + 1]
        slotrow = const[:, C_SLOTROW:C_SLOTROW + CAP]
        tie = const[:, C_TIE:C_TIE + P]
        keepf = const[:, C_KEEPF:C_KEEPF + S]
        keepb = const[:, C_KEEPB:C_KEEPB + S]
        dist = const[:, C_DIST:C_DIST + NT * S]
        onehot = const[0:BUCKETS, C_ONEHOT:C_ONEHOT + 384]
        maskrow = const[0:HEADS, C_MASK:C_MASK + 384]
        xres = sb("xres", [P, NT, D])
        hT = sb("hT", [P, KD, S])
        ybuf = sb("ybuf", [P, NT, D])
        work = sb("work", [P, NT, D])
        cols = sb("cols", [P, A_ROWS + B_ROWS])
        colA = cols[:, 0:A_ROWS]
        colB = cols[:, A_ROWS:A_ROWS + B_ROWS]
        ones = sb("ones", [P, P])
        ones16 = sb("ones16", [P, P], BF16)
        stats = sb("stats", [P, 7, 6])
        eps = sb("eps", [P, 1])
        crep = sb("crep", [P, KD, 32])
        cact = sb("cact", [P, KD])
        modcol = sb("modcol", [P, 3, 4, 4])
        fold = sb("fold", [P, 2, KD])
        sinkbc = sb("sinkbc", [P, 8])
        relb = sb("relb", [BUCKETS, HEADS])
        router = sb("router", [P, KD, EXPERTS])
        lambc = sb("lambc", [P, 4, HD])
        lam = sb("lam", [P, 8])
        mgate = sb("mgate", [P, KD, 16])
        bmg = sb("bmg", [36, 2])

        def view(at, *shape):
            n = int(np.prod(shape))
            assert at + n <= ARENA, (at, shape)
            v = arena[:, at:at + n]
            if len(shape) == 2:
                v = v.rearrange("p (a b) -> p a b", a=shape[0])
            if len(shape) == 3:
                v = v.rearrange("p (a b c) -> p a b c", a=shape[0], b=shape[1])
            return v

        rowsA, rowsB = view(0, P)[0:A_ROWS, :], view(P, P)[0:B_ROWS, :]
        qkT = view(0, 14, S)
        v1 = view(3584, NT, 640)
        biasm = view(4864, HEADS, 384)
        square = view(8192, 2, 512)
        logits = view(11008, 2, 384)
        relu = view(11008, 2, 512)
        G1 = view(12032, D)
        G2 = view(13056, D)
        b2bc = view(14080, D)
        att_s = view(15104, HEADS, 8)
        modrow = view(15232, 3, 512)
        probs = work[:, 0, 0:768].rearrange("p (b n) -> p b n", b=2)
        probsT = work[:, 1, 0:768].rearrange("p (b n) -> p b n", b=2)
        zpad = view(0, 8, S + 4)
        expo = view(0, 2, 1024)
        qkc = view(2080, 8, S)
        conv = view(4128, 2, S)
        vo = view(4640, NT, 2 * MW)
        dqk = view(6688, 8, S)
        dv = view(8736, NT, MW)
        gT = view(9760, 16, S)
        rows2 = view(13856, 8, S)
        comb = view(13856, NT, S)
        combT = view(14368, NT, S)
        rowcols = view(15904, 3, NT, 36)
        unit_s = view(16640, 8, 16)
        mv = view(16768, 16, 2)
        bn6 = view(16800, 16, 6)
        wgi = ybuf[:, 0, 0:KD * 36].rearrange("p (k m) -> p k m", k=KD)
        wgf = ybuf[:, 0, 512:512 + KD * 36].rearrange("p (k m) -> p k m", k=KD)
        mixin = ybuf
        xeT = view(0, KD, EXPERTS * CAP)
        selTg = view(4096, EXPERTS, S)
        affbc = view(8192, EXPERTS, S)
        sel = view(12288, NT, EXPERTS * CAP)
        beats = hT[:, :, :].rearrange("p k s -> p (k s)").bitcast(BF16).rearrange("p (i e t) -> p i e t", i=NT, e=8)
        beats_eq = view(13312, 1024).bitcast(BF16).rearrange("p (i e t) -> p i e t", i=NT, e=8)
        aff = view(14336, NT, EXPERTS)
        rankc = view(14368, NT, EXPERTS)
        aff_s = view(14400, 8)
        xe = view(14464, KD, CAP)
        selx = view(14720, S)
        gfinal = ybuf[:, 0, :]
        silu = view(8192, 512)
        hid = view(8704, 512)
        hidT = view(9216, 4, 4, CAP)
        ye = view(9728, 512)

        PS = ctx.enter_context(nc.psum_tensor("PS", [P, 8, 512], F32))

        loaded = [ctx.enter_context(nc.semaphore(f"loaded{i}")) for i in range(RING_P)]
        expert_loaded = [ctx.enter_context(nc.semaphore(f"expert_loaded{i}")) for i in range(RING)]
        slot_rounded, slot_split_dve, slot_split_pool = sems("slot_rounded slot_split_dve slot_split_pool")
        (slots_used, ident_in, consts_in, x_in, rows_in, late_in, mg_in, ones_set, cols_turned, cols_set, bias_rows, bias_row_set,
         bias_stored, bias_in, bias_copied, c_acted, crep_set, bg_in, gfinal_in) = sems(
            "slots_used ident_in consts_in x_in rows_in late_in mg_in ones_set cols_turned cols_set bias_rows bias_row_set "
            "bias_stored bias_in bias_copied c_acted crep_set bg_in gfinal_in")
        modrow_set, mod_turned, modcol_set, folded, g_spread, g_ready = sems(
            "modrow_set mod_turned modcol_set folded g_spread g_ready")
        dve_chain, act_chain, pool_chain = sems("dve_chain act_chain pool_chain")
        win_out = sems("win_out_dve win_out_act")
        kswap_in, = sems("kswap_in")
        scored, logit_set, negmax_set, exp_set, probs_set, probs_turned, probsT_set, weighed = sems(
            "scored logit_set negmax_set exp_set probs_set probs_turned probsT_set weighed")
        wout_out = sems("wout_out_dve wout_out_act")
        w1_relu, w1_out, w2_out, x1_set, x2_set, x3_set = sems("w1_relu w1_out w2_out x1_set x2_set x3_set")
        mix_out = sems("mix_out_dve mix_out_act")
        (gate_rows, gate_rows_set, gate_exp, gate_ln, gate_m, gate_em, gate_cols, gate_cols_set, pads_set, wg_set,
         bmg_set, conv_set, qk_set, lam_dots, lam_exps, lam_set) = sems(
            "gate_rows gate_rows_set gate_exp gate_ln gate_m gate_em gate_cols gate_cols_set pads_set wg_set "
            "bmg_set conv_set qk_set lam_dots lam_exps lam_set")
        (unit_scored, unit_read, unit_arg, unit_exp, unit_comb, unit_turned, unit_T, unit_out, raw_set,
         gates_out) = sems(
            "unit_scored unit_read unit_arg unit_exp unit_comb unit_turned unit_T unit_out raw_set gates_out")
        osig_set, gsig_set, var2_set, root2_set, mixed = sems(
            "osig_set gsig_set var2_set root2_set mixed")
        (logit16, negmax16, exp16, aff_set, aff_spread, affbc_set, beats_set, rank_spread, rank_cols, selT_set, rankc_set,
         sel_set, gathered, xe_out, acc_started) = sems(
            "logit16 negmax16 exp16 aff_set aff_spread affbc_set beats_set rank_spread rank_cols selT_set rankc_set "
            "sel_set gathered xe_out acc_started")
        xe_ready, selx_ready, silu_set, hid_set, hid_turned, hidT_set, ye_set, scattered = sems(
            "xe_ready selx_ready silu_set hid_set hid_turned hidT_set ye_set scattered")
        final_copied, final_set, out_stored = sems("final_copied final_set out_stored")
        squared, root_set = sems("squared root_set")
        N1, POST1, N2, POST2, N3, N4, NLAST = range(7)
        normed, turned, = sems("normed turned")
        placed = sems("placed_dve placed_act")
        act_rounded, act_split = sems("act_rounded act_split")
        att_rounded, att_split, ff_split = sems("att_rounded att_split ff_split")
        T1, T2, T3, TBRANCH, T4 = range(5)
        TMIXED = 4

        def slot(g):
            return ring[:, g % RING_P, :]

        def arrived(eng, g):
            eng.wait_ge(loaded[g % RING_P], 16 * (g // RING_P + 1))

        def used(g):
            return g + 1

        def pieces(g):
            at = SLOT // 4 if g in BY_POOL else SLOT // 2
            return slice(0, at), slice(at, SLOT)

        def halves(g, part):
            return wR[:, SPLIT.index(g) % 2, part, :]

        def split_done(eng, g):
            by, sem = (BY_POOL, slot_split_pool) if g in BY_POOL else (BY_DVE, slot_split_dve)
            eng.wait_ge(sem, 2 * (by.index(g) + 1))

        def round_slot(eng, g):
            n = SPLIT.index(g)
            arrived(eng, g)
            if n >= 2:
                eng.wait_ge(slots_used, used(SPLIT[n - 2]))
            for piece in pieces(g):
                nc.scalar.activation(halves(g, 0)[:, piece], slot(g)[:, piece], ACT.Copy).then_inc(slot_rounded, 1)

        def residue_slot(eng, by, g):
            n = SPLIT.index(g)
            sem = slot_split_pool if g in BY_POOL else slot_split_dve
            arrived(eng, g)
            for i, piece in enumerate(pieces(g)):
                eng.wait_ge(slot_rounded, 2 * n + i + 1)
                by.tensor_tensor(halves(g, 1)[:, piece], slot(g)[:, piece], halves(g, 0)[:, piece], ALU.subtract)\
                    .then_inc(sem, 1)

        def after(g, k=2):
            return SPLIT[SPLIT.index(g) + k]

        class Chain:
            def __init__(self, eng, sem):
                self.eng, self.sem, self.n = eng, sem, 0

            def __call__(self, instruction):
                self.n += 1
                instruction.then_inc(self.sem, 1)
                self.eng.wait_ge(self.sem, self.n)

        def qk_chunks(chunk):
            v = qkT[:, chunk:chunk + 2, :].rearrange("p m (t s) -> p (m t) s", t=NT)
            return v if chunk in (4, 6) else v[:, :, ::-1]

        def by_rows(w):
            return w.rearrange("(k p) n -> p k n", p=P)

        w_in, w_out, w_ada = by_rows(A["w_in"][0]), by_rows(A["w_out"][0]), A["w_ada"][0]
        w1, w2 = by_rows(A["w1"][0]), by_rows(A["w2"][0])
        w_in2, w_out2 = by_rows(A["w_in_2"][0]), by_rows(A["w_out_2"][0])
        up_a, up_b = by_rows(A["w_up_a_2"][0]), by_rows(A["w_up_b_2"][0])

        def k8(g):
            return slot(g).rearrange("p (k n) -> p k n", k=KD)

        loads = []
        for k in range(8):
            loads.append((slot, w_ada[k * P:(k + 1) * P, 0:SLOT]))
        for i in range(N_WIN):
            loads.append((k8, w_in[:, :, 256 * i:256 * (i + 1)]))
        for r in (1, 2):
            for k in range(8):
                loads.append((slot, w_ada[k * P:(k + 1) * P, r * SLOT:(r + 1) * SLOT]))
        for i in range(N_WOUT):
            loads.append((k8, w_out[:, :, 256 * i:256 * (i + 1)]))
        for half in range(2):
            for i in range(half * MLP_HALF, (half + 1) * MLP_HALF):
                loads.append((k8, w1[:, :, 256 * i:256 * (i + 1)]))
            for i in range(half * MLP_HALF, (half + 1) * MLP_HALF):
                loads.append((lambda g: slot(g).rearrange("p (k n) -> p k n", k=2), w2[:, 2 * i:2 * i + 2, :]))
        mix_cols = [256 * i for i in range(6)] + [DIFF0 + 256 * i for i in range(6)] + [1536, 1792]
        gate_cols0 = DIFF0 + 3 * MW
        for c in mix_cols + [gate_cols0 + 256 * i for i in range(N_GATES2)]:
            loads.append((k8, w_in2[:, :, c:c + 256]))
        for half in range(2):
            for w in (up_a, up_b):
                loads.append((lambda g: slot(g).rearrange("p (k n) -> p k n", k=4), w[:, :, 512 * half:512 * half + 512]))
        for i in range(N_WOUT2):
            loads.append((k8, w_out2[:, :, 256 * i:256 * (i + 1)]))
        assert len(loads) == PRELUDE

        block = ctx.enter_context(nc.Block())

        @block.sync
        def _(sp):
            for g, (dst, src) in enumerate(loads):
                if g >= RING_P:
                    if g - RING_P in SPLIT:
                        split_done(sp, g - RING_P)
                    else:
                        sp.wait_ge(slots_used, used(g - RING_P))
                sp.dma_start(dst(g), src).then_inc(loaded[g % RING_P], 16)
            wg, wu, wd = A["w_gate_e_2"], A["w_up_e_2"], A["w_down_e_2"]
            wg_rows = wg.rearrange("l e (k p) n -> (l e k) p n", p=P)
            wu_rows = wu.rearrange("l e (k p) n -> (l e k) p n", p=P)
            wd_rows = wd.rearrange("l e (k p) n -> (l e k) p n", p=P)
            sp.wait_ge(slots_used, PRELUDE)
            with sp.Fori(0, EXPERTS) as e:
                for r in range(PER_EXPERT):
                    sp.wait_ge(slots_used, e * PER_EXPERT + used(G_EXPERTS + r - RING))
                    if r < 16:
                        rows = (wg_rows, wu_rows)[r // 8]
                        src = rows[bass.ds(e * 8 + r % 8, 1), :, :].rearrange("o p n -> p (o n)")
                        dst = ring[:, r % RING, :]
                    else:
                        src = wd_rows[bass.ds(e * 16 + 2 * (r - 16), 2), :, :].rearrange("o p n -> p o n")
                        dst = ring[:, r % RING, :].rearrange("p (o n) -> p o n", o=2)
                    sp.dma_start(dst, src).then_inc(expert_loaded[r % RING], 16)
            for t in range(NT):
                sp.wait_ge(final_set, t + 1)
                sp.dma_start(out[0, t * P:(t + 1) * P, :], work[:, t, :]).then_inc(out_stored, 16)
            sp.wait_ge(out_stored, 16 * NT)

        @block.tensor
        def _(pe):
            def turn(out_, in_, n=P):
                return nc.tensor.transpose(out_, in_, ident[0:n, 0:n])

            def product(o, weights, tokens, still, start, stop):
                first, second = (weights, tokens) if still == "weights" else (tokens, weights)
                nc.tensor.matmul(o, first[0], second[0], start=start, stop=False)
                nc.tensor.matmul(o, first[0], second[1], start=False, stop=False)
                return nc.tensor.matmul(o, first[1], second[0], start=False, stop=stop)

            def parts(g, k):
                split_done(pe, g)
                return [halves(g, part).rearrange("p (k n) -> p k n", k=k) for part in range(2)]

            def channels_out(o, w, cols, acts, ks):
                for n, (kw, ka) in enumerate(ks):
                    mm = product(o, [x[:, kw, cols] for x in w], [acts[:, part, ka, :] for part in range(2)], "weights",
                                 n == 0, n == len(ks) - 1)
                return mm

            def tokens_out(o, w, cols, t):
                for k in range(KD):
                    mm = product(o, [x[:, k, cols] for x in w], [hR[:, part, k, t * P:(t + 1) * P] for part in range(2)],
                                 "tokens", k == 0, k == KD - 1)
                return mm

            ALL_K = [(k, k) for k in range(KD)]

            def weights_still(g, bank):
                w = parts(g, KD)
                for m in range(2):
                    mm = channels_out(PS[:, bank, m * S:(m + 1) * S], w, slice(m * P, (m + 1) * P), hR, ALL_K)
                mm.then_inc(slots_used, 1)

            def tokens_still(g, bank):
                w = parts(g, KD)
                for t in range(NT):
                    mm = tokens_out(PS[:, bank, t * 256:(t + 1) * 256], w, slice(0, 256), t)
                mm.then_inc(slots_used, 1)

            def turn_tiles(n, src, base):
                for t in range(NT):
                    pe.wait_ge(normed, 2 * n + t + 1)
                    for k in range(KD):
                        mm = turn(PS[:, base + 2 * t + k // 4, (k % 4) * P:(k % 4 + 1) * P],
                                  src[:, t, k * P:(k + 1) * P])
                        if k % 4 == 3:
                            mm.then_inc(turned, 1)

            pe.wait_ge(ident_in, 16)
            pe.wait_ge(rows_in, 16 * 10)
            turn(PS[:, 0, 0:A_ROWS], rowsA[:, :], A_ROWS)
            turn(PS[:, 0, A_ROWS:A_ROWS + B_ROWS], rowsB[:, :], B_ROWS).then_inc(cols_turned, 1)
            def ada(g, k, bank):
                arrived(pe, g)
                for j in range(4):
                    mm = nc.tensor.matmul(PS[32 * j:32 * j + 32, bank, :], crep[:, k, :],
                                          slot(g)[:, 512 * j:512 * (j + 1)], start=(k == 0), stop=(k == 7),
                                          tile_position=(0, 32 * j))
                mm.then_inc(slots_used, 1)

            def turn_mod(r, bank):
                for q in range(4):
                    mm = turn(PS[:, bank, q * P:(q + 1) * P], modrow[:, r, q * P:(q + 1) * P])
                mm.then_inc(mod_turned, 1)

            pe.wait_ge(crep_set, 1)
            for k in range(8):
                ada(G_ADA0 + k, k, 2)
                if k == 4:
                    pe.wait_ge(consts_in, 16 * 2)
                    nc.tensor.matmul(PS[0:HEADS, 1, 0:384], relb[:, :], onehot, start=True, stop=True)\
                        .then_inc(bias_rows, 1)
            pe.wait_ge(modrow_set, 1)
            turn_mod(0, 3)
            turn_tiles(T1, work, 4)
            pe.wait_ge(act_split, 2 * T1 + 2)
            pe.wait_ge(bias_row_set, 1)
            for i in range(N_WIN):
                if i >= 4:
                    pe.wait_ge(win_out[i % 2], (i - 4) // 2 + 1)
                g = G_WIN + i
                if i in (2 * 2, 2 * 2 + 1):
                    tokens_still(g, i % 4)
                elif i < 8:
                    weights_still(g, i % 4)
                else:
                    w = parts(g, KD)
                    channels_out(PS[:, 0, 0:S], w, slice(0, P), hR, ALL_K)
                    for t in range(NT):
                        mm = tokens_out(PS[:, 0, S + t * P:S + (t + 1) * P], w, slice(P, 2 * P), t)
                    mm.then_inc(slots_used, 1)

            def heads_qkv(h):
                if h < 8:
                    r = 64 * (h % 2)
                    return r, qkT[r:r + HD, h // 2, :], qkT[r:r + HD, 4 + h // 2, :], h * HD
                j = h - 8
                r = 64 * (j % 2)
                kv = j // 4
                kchunk = 12 if kv == j % 2 else 13
                return r, qkT[r:r + HD, 8 + j // 2, :], qkT[r:r + HD, kchunk, :], W_A + kv * HD

            def score(h):
                r, q, k, _ = heads_qkv(h)
                if h == 8:
                    pe.wait_ge(kswap_in, 32)
                if h >= 2:
                    pe.wait_ge(logit_set, h - 1)
                nc.tensor.matmul(PS[:, h % 2, 0:S], q[:, P:S], k[:, :], start=True, stop=True)
                nc.tensor.matmul(PS[:, h % 2, S:S + P], q[:, 0:P], k[:, 0:P], start=True, stop=True)\
                    .then_inc(scored, 1)

            def turn_probs(h):
                pe.wait_ge(probs_set, h + 1)
                if h >= 2:
                    pe.wait_ge(probsT_set, h - 1)
                b = 2 + h % 2
                turn(PS[:, b, 0:P], probs[:, h % 2, S:S + P])
                turn(PS[:, b, P:S], probs[:, h % 2, 0:P])
                turn(PS[:, b, S:S + P], probs[:, h % 2, P:S]).then_inc(probs_turned, 1)

            def weigh(h):
                r, _, _, c = heads_qkv(h)
                pe.wait_ge(probsT_set, h + 1)
                if h % 2 == 0 and h >= 4:
                    pe.wait_ge(att_split, h // 2 - 1)
                o = PS[r:r + HD, 4 + (h // 2) % 2, :]
                nc.tensor.matmul(o[:, 0:S], v1[:, 0, c:c + HD], probsT[:, h % 2, 0:S], start=True, stop=False)
                nc.tensor.matmul(o[:, P:S], v1[:, 1, c:c + HD], probsT[:, h % 2, S:S + P], start=False, stop=True)\
                    .then_inc(weighed, 1)

            pe.wait_ge(win_out[0], 5)
            pe.wait_ge(win_out[1], 4)
            for h in range(HEADS + 2):
                if h < HEADS:
                    score(h)
                    ada(G_ADA12 + h, h % 8, 6 + h // 8)
                if 1 <= h <= HEADS:
                    turn_probs(h - 1)
                if h >= 2:
                    weigh(h - 2)
            pe.wait_ge(modrow_set, 3)
            pe.wait_ge(logit_set, HEADS)
            turn_mod(1, 0)
            turn_mod(2, 1)
            pe.wait_ge(probsT_set, HEADS)
            for n, (r, j, bank) in enumerate([(1, 0, 2), (1, 1, 3), (2, 2, 6), (2, 3, 7)]):
                nc.tensor.matmul(PS[:, bank, :], ones[32 * j:32 * j + 1, :], modrow[32 * j:32 * j + 1, r, :],
                                 start=True, stop=True, tile_position=(32 * j, 0)).then_inc(g_spread, 1)
            pe.wait_ge(att_split, HEADS // 2)
            pe.wait_ge(modcol_set, 3)
            pe.wait_ge(g_ready, 4)
            for i in range(N_WOUT):
                tokens_still(G_WOUT + i, i)

            turn_tiles(T2, work, 4)
            pe.wait_ge(act_split, 2 * T2 + 2)
            for half in range(2):
                these = range(half * MLP_HALF, (half + 1) * MLP_HALF)
                for i in these:
                    if i >= 4:
                        pe.wait_ge(w1_relu, 2 * (i - 3))
                    weights_still(g_w1(i), i % 4)
                for i in these:
                    pe.wait_ge(ff_split, i + 1)
                    w = parts(g_w2(i), 2)
                    for a in range(2):
                        for t in range(NT):
                            for c in range(2):
                                mm = product(PS[:, 4 + 2 * t + c, :], [x[:, a, 512 * c:512 * (c + 1)] for x in w],
                                             [fR[:, part, 2 * (i % MLP_HALF) + a, t * P:(t + 1) * P] for part in range(2)],
                                             "tokens", i == 0 and a == 0, i == N_W2 - 1 and a == 1)
                    mm.then_inc(slots_used, 1)

            turn_tiles(T3, work, 0)
            pe.wait_ge(act_split, 2 * T3 + 2)
            pe.wait_ge(wg_set, 4)
            for part, w in enumerate((wgi, wgf)):
                for k in range(KD):
                    mm = nc.tensor.matmul(PS[0:36, 4, part * S:(part + 1) * S], w[:, k, :], hT[:, k, :],
                                          start=(k == 0), stop=(k == KD - 1))
            mm.then_inc(gate_rows, 1)
            for i in range(N_MIX2):
                if i >= 4:
                    pe.wait_ge(mix_out[i % 2], (i - 4) // 2 + 1)
                if i in (4, 5, 10, 11, 12, 13):
                    tokens_still(G_MIX2 + i, i % 4)
                else:
                    weights_still(G_MIX2 + i, i % 4)
                if i == 8:
                    pe.wait_ge(gate_em, 1)
                    for n, row in enumerate((4, 5, 7)):
                        for t in range(NT):
                            mm = turn(PS[:, 5, (2 * n + t) * 36:(2 * n + t + 1) * 36],
                                      rows2[0:36, row, t * P:(t + 1) * P], 36)
                    mm.then_inc(gate_cols, 1)

            def unit_scores(u):
                b = 2 * (u % 2)
                if u >= 2:
                    pe.wait_ge(unit_read, u - 1)
                if u < MH:
                    for t in range(NT):
                        nc.tensor.matmul(PS[:, b, t * S:(t + 1) * S], qkc[:, u, t * P:(t + 1) * P], qkc[:, 4 + u, :],
                                         start=True, stop=True)
                    for d in range(2):
                        for t in range(NT):
                            c = rowcols[:, 0, t, 32 * d + u:32 * d + u + 1]
                            mm = turn(PS[:, b + 1, d * S + t * P:d * S + (t + 1) * P], c.to_broadcast([P, P]))
                else:
                    h = u - MH
                    for t in range(NT):
                        for c in range(2):
                            mm = nc.tensor.matmul(PS[:, b + c, t * S:(t + 1) * S],
                                                  dqk[64 * c:64 * c + HD, h, t * P:(t + 1) * P],
                                                  dqk[64 * c:64 * c + HD, 4 + h, :], start=True, stop=True)
                mm.then_inc(unit_scored, 1)

            def unit_turn(u):
                pe.wait_ge(unit_comb, u + 1)
                if u >= 1:
                    pe.wait_ge(unit_T, u)
                for j in range(NT):
                    for t in range(NT):
                        mm = turn(PS[:, 4, j * S + t * P:j * S + (t + 1) * P], comb[:, t, j * P:(j + 1) * P])
                mm.then_inc(unit_turned, 1)

            def unit_values(u):
                pe.wait_ge(unit_T, u + 1)
                if u >= 1:
                    pe.wait_ge(raw_set, u)
                v = vo if u < MH else dv
                c = (u % MH) * P
                for t in range(NT):
                    for j in range(NT):
                        mm = nc.tensor.matmul(PS[:, 5, t * P:(t + 1) * P], combT[:, j, t * P:(t + 1) * P],
                                              v[:, j, c:c + P], start=(j == 0), stop=(j == NT - 1))
                mm.then_inc(unit_out, 1)

            pe.wait_ge(mix_out[0], N_MIX2 // 2)
            pe.wait_ge(mix_out[1], N_MIX2 // 2)
            pe.wait_ge(qk_set, 8)
            pe.wait_ge(gate_cols_set, 1)
            unit_scores(0)
            for u in range(2 * MH + 1):
                if u + 1 < 2 * MH:
                    unit_scores(u + 1)
                if u >= 1:
                    unit_turn(u - 1)
                if u < 2 * MH:
                    if u >= 2:
                        pe.wait_ge(gates_out, u - 1)
                    weights_still(G_GATES2 + u, 6 + u % 2)
                if u >= 1:
                    unit_values(u - 1)

            turn_tiles(TBRANCH, work, 0)
            pe.wait_ge(act_split, 2 * TBRANCH + 2)
            pe.wait_ge(raw_set, 8)
            pe.wait_ge(gates_out, 8)
            for i in range(N_UP):
                w = parts(G_UP + i, 4)
                for m in range(4):
                    mm = channels_out(PS[:, 2 * i + m // 2, (m % 2) * S:(m % 2 + 1) * S], w, slice(m * P, (m + 1) * P), hR,
                                      [(k, 4 * (i % 2) + k) for k in range(4)])
                mm.then_inc(slots_used, 1)
            pe.wait_ge(act_split, 2 * TMIXED + 2)
            for i in range(N_WOUT2):
                tokens_still(G_WOUT2 + i, i)

            turn_tiles(T4, work, 4)
            pe.wait_ge(placed[0], 2 * T4 + 2)
            pe.wait_ge(placed[1], 2 * T4 + 2)
            for t in range(NT):
                for k in range(KD):
                    mm = nc.tensor.matmul(PS[:, 0, t * EXPERTS:(t + 1) * EXPERTS], hT[:, k, t * P:(t + 1) * P],
                                          router[:, k, :], start=(k == 0), stop=(k == KD - 1))
            mm.then_inc(logit16, 1)
            pe.wait_ge(aff_set, 1)

            def spread(q):
                if q >= 2:
                    pe.wait_ge(affbc_set, q - 1)
                for e in range(4):
                    for t in range(NT):
                        mm = turn(PS[:, 2 * (q % 2) + e // 2, (e % 2) * S + t * P:(e % 2) * S + (t + 1) * P],
                                  aff[:, t, 4 * q + e:4 * q + e + 1].to_broadcast([P, P]))
                mm.then_inc(aff_spread, 1)

            def count(q):
                e0 = 2 * (q % 4)
                bank = 4 + q % 2
                if q >= 2:
                    pe.wait_ge(selT_set, q - 1)
                for i in range(NT):
                    nc.tensor.matmul(PS[:, bank, :], ones16[:, :], beats[:, i, e0:e0 + 2, :].rearrange("p e t -> p (e t)"),
                                     start=(i == 0), stop=False, skip_group_check=True)
                o = PS[:, bank, :].rearrange("p (e t) -> p e t", e=2)
                for i in range(NT):
                    mm = nc.tensor.matmul(o[:, :, i * P:(i + 1) * P], ones16[:, :], beats_eq[:, i, e0:e0 + 2, :],
                                          start=False, stop=(i == NT - 1), skip_group_check=True)
                mm.then_inc(rank_spread, 1)
                for e in range(2):
                    for t in range(NT):
                        o = PS[:, 6, t * EXPERTS + 2 * q + e:t * EXPERTS + 2 * q + e + 1]
                        for i in range(NT):
                            nc.tensor.matmul(o, beats[:, i, e0 + e, t * P:(t + 1) * P], ones16[:, 0:1],
                                             start=(i == 0), stop=False)
                        mm = nc.tensor.matmul(o, beats_eq[:, t, e0 + e, :], ones16[:, 0:1], start=False, stop=True)
                mm.then_inc(rank_cols, 1)

            spread(0)
            for q in range(4):
                if q + 1 < 4:
                    spread(q + 1)
                pe.wait_ge(beats_set, q + 1)
                count(2 * q)
                count(2 * q + 1)
            pe.wait_ge(sel_set, 2)
            pe.wait_ge(affbc_set, 4)
            for k in range(KD):
                if k >= 4:
                    pe.wait_ge(xe_out, k - 3)
                for t in range(NT):
                    mm = nc.tensor.matmul(PS[:, k % 4, :], work[:, t, k * P:(k + 1) * P], sel[:, t, :],
                                          start=(t == 0), stop=(t == NT - 1))
                mm.then_inc(gathered, 1)
            pe.wait_ge(selT_set, 8)
            pe.wait_ge(rankc_set, 1)
            for t in range(NT):
                for half in range(2):
                    mm = nc.tensor.matmul(PS[:, 4 + 2 * t + half, :], ident, xres[:, t, 512 * half:512 * (half + 1)],
                                          start=True, stop=False, skip_group_check=True)
            mm.then_inc(scattered, 1)
            pe.wait_ge(xe_out, KD)

            with pe.Fori(0, EXPERTS) as e:
                pe.wait_ge(xe_ready, e + 1)
                for r in range(16):
                    pe.wait_ge(expert_loaded[r % RING], e * 32 + 16 * (r // RING + 1))
                    for j in range(4):
                        mm = nc.tensor.matmul(PS[32 * j:32 * j + 32, r // 8, :], xe[:, r % 8, :],
                                              ring[:, r % RING, 512 * j:512 * (j + 1)], start=(r % 8 == 0),
                                              stop=(r % 8 == 7), tile_position=(0, 32 * j))
                    mm.then_inc(slots_used, 1)
                pe.wait_ge(hid_set, e + 1)
                for c in range(4):
                    mm = turn(PS[:, 2, c * P:(c + 1) * P], hid[:, c * P:(c + 1) * P])
                mm.then_inc(hid_turned, 1)
                pe.wait_ge(hidT_set, e + 1)
                for r in range(16, 24):
                    pe.wait_ge(expert_loaded[r % RING], e * 32 + 16 * (r // RING + 1))
                    w = ring[:, r % RING, :].rearrange("p (a n) -> p a n", a=2)
                    for half in range(2):
                        for a in range(2):
                            chunk = 2 * (r - 16) + a
                            q = 2 * half + a
                            mm = nc.tensor.matmul(PS[32 * q:32 * q + 32, 3, :], hidT[:, chunk % 4, chunk // 4, :],
                                                  w[:, a, 512 * half:512 * (half + 1)], start=(r == 16),
                                                  stop=(r == 23), tile_position=(0, 32 * q))
                    mm.then_inc(slots_used, 1)
                pe.wait_ge(selx_ready, e + 1)
                pe.wait_ge(ye_set, e + 1)
                for t in range(NT):
                    for half in range(2):
                        mm = nc.tensor.matmul(PS[:, 4 + 2 * t + half, :], selx[64 * half:64 * half + 64, t * P:(t + 1) * P],
                                              ye[64 * half:64 * half + 64, :], start=False, stop=False,
                                              skip_group_check=True, tile_position=(64 * half, 0))
                mm.then_inc(scattered, 1)

        @block.vector
        def _(dve):
            V = nc.vector
            then = Chain(dve, dve_chain)

            def factor(n, t):
                dve.wait_ge(root_set, 2 * n + t + 1)
                then(V.reciprocal(stats[:, n, 4 + t:5 + t], stats[:, n, 2 + t:3 + t]))
                return stats[:, n, 4 + t:5 + t]

            def norm(n):
                for t in range(NT):
                    V.tensor_scalar(work[:, t, :], xres[:, t, :], factor(n, t), None, ALU.mult).then_inc(normed, 1)

            def place(n, base, dst, scale, shift):
                for j in (0, 2):
                    dve.wait_ge(turned, 4 * n + j + 1)
                    for q in range(4):
                        k = 4 * (j % 2) + q
                        o, i = dst[:, k, (j // 2) * P:(j // 2 + 1) * P], PS[:, base + j, q * P:(q + 1) * P]
                        if shift is None:
                            last = V.tensor_scalar(o, i, scale(k), None, ALU.mult)
                        else:
                            last = V.tensor_scalar(o, i, scale(k), shift(k), ALU.mult, ALU.add)
                    last.then_inc(placed[0], 1)

            def residue_act(n, src):
                for t in range(NT):
                    tile = slice(t * P, (t + 1) * P)
                    dve.wait_ge(act_rounded, 2 * n + t + 1)
                    V.tensor_tensor(hR[:, 1, :, tile], src[:, :, tile], hR[:, 0, :, tile], ALU.subtract)\
                        .then_inc(act_split, 1)

            V.memset(ones[:, :], 1.0).then_inc(ones_set, 1)
            V.memset(ones16[:, :], 1.0).then_inc(ones_set, 1)
            V.memset(eps[:, :], EPS).then_inc(ones_set, 1)
            V.memset(bmg[:, :], 0.0).then_inc(bmg_set, 1)
            dve.wait_ge(cols_turned, 1)
            V.tensor_copy(cols[:, :], PS[:, 0, 0:A_ROWS + B_ROWS]).then_inc(cols_set, 1)
            dve.wait_ge(c_acted, 1)
            V.tensor_copy(crep[:, :, :], cact[:, :].unsqueeze(2).to_broadcast([P, KD, 32])).then_inc(crep_set, 1)

            norm(N1)

            def mod_columns(r, bank):
                dve.wait_ge(mod_turned, r + 1)
                V.tensor_tensor(modcol[:, r, :, :], PS[:, bank, :].rearrange("p (q j i) -> p j q i", q=4, j=4)[:, :, :, 0],
                                colA[:, A_BADA + 16 * r:A_BADA + 16 * (r + 1)].rearrange("p (j q) -> p j q", j=4),
                                ALU.add).then_inc(modcol_set, 1)
                dve.wait_ge(modcol_set, r + 1)

            def fold_gain(n, gain, scale):
                then(V.tensor_scalar(fold[:, n, :], scale, 1.0, None, ALU.add))
                V.tensor_tensor(fold[:, n, :], fold[:, n, :], colA[:, A_GAIN + 8 * gain:A_GAIN + 8 * gain + 8], ALU.mult)\
                    .then_inc(folded, 1)
                dve.wait_ge(folded, n + 1)

            dve.wait_ge(bias_rows, 1)
            V.tensor_tensor(logits[0:HEADS, 0, :], PS[0:HEADS, 1, 0:384], maskrow, ALU.add).then_inc(bias_row_set, 1)
            for g in range(G_WIN, G_WIN + 2):
                residue_slot(dve, V, g)
            dve.wait_ge(slots_used, used(G_ADA0 + 7))
            V.tensor_copy(modrow[:, 0, :], PS[:, 2, :]).then_inc(modrow_set, 1)
            mod_columns(0, 3)
            shift1 = modcol[:, 0, 0:2, :].rearrange("p j q -> p (j q)")
            scale1 = modcol[:, 0, 2:4, :].rearrange("p j q -> p (j q)")
            fold_gain(0, 0, scale1)
            place(T1, 4, hT, lambda k: fold[:, 0, k:k + 1], lambda k: shift1[:, k:k + 1])
            residue_act(T1, hT)

            for i in range(N_WIN):
                if i + 2 < N_WIN:
                    residue_slot(dve, V, G_WIN + i + 2)
                if i % 2:
                    continue
                dve.wait_ge(slots_used, used(G_WIN + i))
                if i < 8:
                    if i == 4:
                        V.tensor_copy(v1[:, :, 0:256], PS[:, i % 4, :].rearrange("p (t n) -> p t n", t=NT))\
                            .then_inc(win_out[0], 1)
                    else:
                        chunk = {0: 0, 2: 4, 6: 8}[i]
                        V.tensor_copy(qk_chunks(chunk), PS[:, i % 4, :].rearrange("p (m s) -> p m s", m=4))\
                            .then_inc(win_out[0], 1)
                else:
                    V.tensor_copy(qkT[:, 12, :], PS[:, 0, 0:S])
                    V.tensor_copy(v1[:, :, W_A:W_A + P], PS[:, 0, S:2 * S].rearrange("p (t n) -> p t n", t=NT))\
                        .then_inc(win_out[0], 1)

            def att_residue(pair):
                dve.wait_ge(att_rounded, pair + 1)
                V.tensor_tensor(hR[:, 1, pair, :], PS[:, 4 + pair % 2, 0:S], hR[:, 0, pair, :], ALU.subtract)\
                    .then_inc(att_split, 1)

            dve.wait_ge(late_in, 16 * 6)
            then(V.tensor_tensor(lambc[:, 0, :], lambc[:, 0, :], lambc[:, 1, :], ALU.mult))
            then(V.tensor_tensor(lambc[:, 2, :], lambc[:, 2, :], lambc[:, 3, :], ALU.mult))
            V.tensor_reduce(lam[:, 0:1], lambc[:, 0, :], AX_X, ALU.add)
            V.tensor_reduce(lam[:, 1:2], lambc[:, 2, :], AX_X, ALU.add).then_inc(lam_dots, 1)
            dve.wait_ge(bias_copied, 1)
            for h in range(HEADS + 2):
                if h < HEADS:
                    s = att_s[:, h, :]
                    L = logits[:, h % 2, :]
                    dve.wait_ge(scored, h + 1)
                    if h >= 2:
                        dve.wait_ge(exp_set, h - 1)
                    V.scalar_tensor_tensor(L, PS[:, h % 2, 0:384], HD ** -0.5, biasm[:, h, :], ALU.mult, ALU.add)\
                        .then_inc(logit_set, 1)
                    dve.wait_ge(logit_set, h + 1)
                    V.tensor_reduce(s[:, 0:1], L[:, 0:S], AX_X, ALU.max)
                    then(V.tensor_reduce(s[:, 1:2], L[:, S:384], AX_X, ALU.max))
                    sink = sinkbc[:, h - 8:h - 7] if h >= 8 else -BIG
                    V.tensor_scalar(s[:, 0:2], s[:, 0:2], sink, -1.0, ALU.max, ALU.mult).then_inc(negmax_set, 1)
                if 1 <= h <= HEADS:
                    g = h - 1
                    s = att_s[:, g, :]
                    dve.wait_ge(exp_set, g + 1)
                    if g >= 8:
                        then(V.tensor_tensor(s[:, 2:4], s[:, 2:4], s[:, 4:6], ALU.add))
                    then(V.reciprocal(s[:, 6:8], s[:, 2:4]))
                    V.tensor_scalar(probs[:, g % 2, 0:S], probs[:, g % 2, 0:S], s[:, 6:7], None, ALU.mult)
                    V.tensor_scalar(probs[:, g % 2, S:384], probs[:, g % 2, S:384], s[:, 7:8], None, ALU.mult)\
                        .then_inc(probs_set, 1)
                    if g == 7:
                        dve.wait_ge(slots_used, used(G_ADA12 + 7))
                        V.tensor_copy(modrow[:, 1, :], PS[:, 6, :]).then_inc(modrow_set, 1)
                if h >= 3 and h % 2 == 1:
                    att_residue(h // 2 - 1)
            dve.wait_ge(slots_used, used(G_ADA12 + 15))
            V.tensor_copy(modrow[:, 2, :], PS[:, 7, :]).then_inc(modrow_set, 1)
            dve.wait_ge(lam_exps, 1)
            then(V.tensor_tensor(lam[:, 4:5], lam[:, 3:4], lam[:, 2:3], ALU.subtract))
            V.tensor_scalar(lam[:, 5:6], lam[:, 4:5], -LAM_INIT, None, ALU.add).then_inc(lam_set, 1)
            mod_columns(1, 0)
            mod_columns(2, 1)
            fold_gain(1, 2, modcol[:, 2, 0:2, :].rearrange("p j q -> p (j q)"))
            dve.wait_ge(bg_in, 16 * 2)
            for n, bank in enumerate((2, 3, 6, 7)):
                half = slice(512 * (n % 2), 512 * (n % 2) + 512)
                G, bg = (G1, G2)[n // 2], ybuf[:, n // 2, half]
                dve.wait_ge(g_spread, n + 1)
                then(V.tensor_tensor(bg, PS[:, bank, :], bg, ALU.add))
                V.tensor_tensor(G[:, half], G[:, half], bg, ALU.mult).then_inc(g_ready, 1)
            dve.wait_ge(g_ready, 4)
            for g in range(G_WOUT, G_WOUT + 2):
                residue_slot(dve, V, g)

            def post_norm(n, G, done):
                for t in range(NT):
                    then(V.scalar_tensor_tensor(work[:, t, :], ybuf[:, t, :], factor(n, t), G, ALU.mult, ALU.mult))
                    V.tensor_tensor(xres[:, t, :], xres[:, t, :], work[:, t, :], ALU.add).then_inc(done, 1)

            for i in range(N_WOUT):
                if i < 3:
                    residue_slot(dve, V, after(G_WOUT + i))
                if i % 2:
                    continue
                dve.wait_ge(slots_used, used(G_WOUT + i))
                V.tensor_copy(ybuf[:, :, 256 * i:256 * (i + 1)], PS[:, i, :].rearrange("p (t n) -> p t n", t=NT))\
                    .then_inc(wout_out[0], 1)
            post_norm(POST1, G1, x1_set)
            dve.wait_ge(x1_set, 2)
            norm(N2)
            shift2 = modcol[:, 1, 2:4, :].rearrange("p j q -> p (j q)")
            place(T2, 4, hT, lambda k: fold[:, 1, k:k + 1], lambda k: shift2[:, k:k + 1])
            residue_act(T2, hT)
            residue_slot(dve, V, G_MLP + 1)
            for half in range(2):
                for i in range(half * MLP_HALF, (half + 1) * MLP_HALF):
                    dve.wait_ge(slots_used, used(g_w1(i)))
                    if i >= 2:
                        dve.wait_ge(w1_out, i - 1)
                    for m in range(2):
                        c = 2 * i + m
                        V.tensor_scalar(relu[:, i % 2, m * S:(m + 1) * S], PS[:, i % 4, m * S:(m + 1) * S],
                                        colA[:, A_B1 + c:A_B1 + c + 1], 0.0, ALU.add, ALU.max).then_inc(w1_relu, 1)
                    residue_slot(dve, V, after(g_w1(i)))
                    dve.wait_ge(w1_out, i + 1)
                    c = 2 * (i % MLP_HALF)
                    V.tensor_tensor(fR[:, 1, c:c + 2, :].rearrange("p m s -> p (m s)"), square[:, i % 2, :],
                                    fR[:, 0, c:c + 2, :].rearrange("p m s -> p (m s)"), ALU.subtract).then_inc(ff_split, 1)
                for i in range(half * MLP_HALF, (half + 1) * MLP_HALF):
                    if g_w2(i) < G_MIX2 - 2:
                        residue_slot(dve, V, after(g_w2(i)))
            dve.wait_ge(slots_used, used(G_MIX2 - 1))
            for t in range(NT):
                V.tensor_tensor(ybuf[:, t, :], PS[:, 4 + 2 * t:6 + 2 * t, :].rearrange("p b n -> p (b n)"), b2bc, ALU.add)\
                    .then_inc(w2_out, 1)
            post_norm(POST2, G2, x2_set)
            dve.wait_ge(x2_set, 2)
            norm(N3)
            place(T3, 0, hT, lambda k: colB[:, B_NMIX + k:B_NMIX + k + 1], None)
            residue_act(T3, hT)

            def gate_rows_program():
                R = rows2[0:36, :, :]
                dve.wait_ge(gate_rows, 1)
                dve.wait_ge(mg_in, 16 * 5)
                dve.wait_ge(pads_set, 2)
                V.tensor_scalar(R[:, 0, :], PS[0:36, 4, 0:S], bmg[:, 0:1], None, ALU.add)
                then(V.tensor_scalar(R[:, 1, :], PS[0:36, 4, S:2 * S], bmg[:, 1:2], None, ALU.add))
                V.scalar_tensor_tensor(R[:, 2, :], R[:, 1, :], -1.0, R[:, 1, :], ALU.mult, ALU.min).then_inc(gate_rows_set, 1)
                dve.wait_ge(gate_ln, 1)
                then(V.scalar_tensor_tensor(R[:, 2, :], R[:, 1, :], 0.0, R[:, 2, :], ALU.min, ALU.subtract))
                zero = R[:, 6, :]
                for part, way in ((0, 1), (32, -1)):
                    r = rows2[part:part + 4, :, :]
                    ze = zero[part:part + 4, :]
                    then(V.tensor_tensor_scan(r[:, 3, ::way], r[:, 2, ::way], ze, 0.0, ALU.add, ALU.add))
                    then(V.tensor_tensor(r[:, 4, :], r[:, 0, :], r[:, 3, :], ALU.subtract))
                    then(V.tensor_tensor_scan(r[:, 5, ::way], r[:, 4, ::way], ze, 0.0, ALU.max, ALU.add))
                    V.tensor_tensor(r[:, 7, :], r[:, 3, :], r[:, 5, :], ALU.add).then_inc(gate_m, 1)

            def convolve(c):
                if c >= 2:
                    dve.wait_ge(qk_set, c - 1)
                a = conv[:, c % 2, :]
                then(V.tensor_scalar(a, zpad[:, c, 0:S], colB[:, B_CONVW + c:B_CONVW + c + 1],
                                     colB[:, B_CONVB + c:B_CONVB + c + 1], ALU.mult, ALU.add))
                for j in range(1, 5):
                    w = colB[:, B_CONVW + 8 * j + c:B_CONVW + 8 * j + c + 1]
                    ins = V.scalar_tensor_tensor(a, zpad[:, c, j:j + S], w, a, ALU.mult, ALU.add)
                    if j < 4:
                        then(ins)
                ins.then_inc(conv_set, 1)

            for i in range(N_MIX2):
                if i in range(4, 4 + 8):
                    if i == 4:
                        dve.wait_ge(mix_out[0], 2)
                        dve.wait_ge(mix_out[1], 2)
                    convolve(i - 4)
                if i % 2:
                    continue
                dve.wait_ge(slots_used, used(G_MIX2 + i))
                turned_ = PS[:, i % 4, :].rearrange("p (m s) -> p m s", m=2)
                tokens_ = PS[:, i % 4, :].rearrange("p (t n) -> p t n", t=NT)
                if i == 0:
                    dve.wait_ge(pads_set, 2)
                if i < 4:
                    last = V.tensor_copy(zpad[:, 2 * i:2 * i + 2, 2:2 + S], turned_)
                elif i == 4:
                    last = V.tensor_copy(vo[:, :, 0:256], tokens_)
                elif i < 10:
                    last = V.tensor_copy(dqk[:, 2 * (i - 6):2 * (i - 6) + 2, :], turned_)
                elif i == 10:
                    last = V.tensor_copy(dv[:, :, 0:256], tokens_)
                else:
                    last = V.tensor_copy(vo[:, :, MW:MW + 256], tokens_)
                last.then_inc(mix_out[0], 1)
                if i == 2:
                    gate_rows_program()
                if i == 8:
                    dve.wait_ge(gate_cols, 1)
                    V.tensor_copy(rowcols[:, :, :, :], PS[:, 5, 0:216].rearrange("p (n t m) -> p n t m", n=3, t=NT))\
                        .then_inc(gate_cols_set, 1)

            def mlstm_args(u):
                b, E = 2 * (u % 2), expo[:, u % 2, :]
                M = lambda d, t: rowcols[:, 1, t, 32 * d + u:32 * d + u + 1]
                f, w = PS[:, b + 1, 0:S], PS[:, b + 1, S:2 * S]
                V.scalar_tensor_tensor(E[:, 0:256], f, M(0, 1), keepf, ALU.subtract, ALU.min)
                V.scalar_tensor_tensor(E[:, 256:512], w, M(1, 0), keepb, ALU.subtract, ALU.min)
                V.scalar_tensor_tensor(E[:, 512:640], f[:, 0:P], M(0, 0), keepf[:, P:S], ALU.subtract, ALU.min)
                V.scalar_tensor_tensor(E[:, 640:768], w[:, P:S], M(1, 1), keepb[:, 0:P], ALU.subtract, ALU.min)\
                    .then_inc(unit_arg, 1)

            def mlstm_combine(u):
                b, E, s = 2 * (u % 2), expo[:, u % 2, :], unit_s[:, u, :]
                dve.wait_ge(unit_exp, u + 1)
                for n, (o, c, z) in enumerate([(0, 256, 256), (256, 0, 256), (512, 0, 128), (640, 384, 128)]):
                    last = V.scalar_tensor_tensor(E[:, o:o + z], PS[:, b, c:c + z], P ** -0.5, E[:, o:o + z], ALU.mult,
                                                  ALU.mult, accum_out=s[:, n:n + 1])
                last.then_inc(unit_read, 1)
                dve.wait_ge(unit_read, u + 1)
                then(V.scalar_tensor_tensor(s[:, 12:16], s[:, 0:4], -1.0, s[:, 0:4], ALU.mult, ALU.max))
                for n, (d, t) in enumerate([(0, 1), (1, 0), (0, 0), (1, 1)]):
                    last = V.tensor_tensor(s[:, 4 + n:5 + n], s[:, 12 + n:13 + n],
                                           rowcols[:, 2, t, 32 * d + u:32 * d + u + 1], ALU.max)
                then(last)
                then(V.reciprocal(s[:, 8:12], s[:, 4:8]))
                if u >= 1:
                    dve.wait_ge(unit_turned, u)
                then(V.tensor_scalar(comb[:, 1, :], E[:, 0:256], s[:, 8:9], None, ALU.mult))
                then(V.tensor_scalar(comb[:, 0, :], E[:, 256:512], s[:, 9:10], None, ALU.mult))
                V.scalar_tensor_tensor(comb[:, 0, 0:P], E[:, 512:640], s[:, 10:11], comb[:, 0, 0:P], ALU.mult, ALU.add)
                V.scalar_tensor_tensor(comb[:, 1, P:S], E[:, 640:768], s[:, 11:12], comb[:, 1, P:S], ALU.mult, ALU.add)\
                    .then_inc(unit_comb, 1)

            def diff_args(u):
                b, E, s = 2 * (u % 2), expo[:, u % 2, :], unit_s[:, u, :]
                slope = 2.0 ** (-8.0 * (u - MH + 1) / MH)
                for t in range(NT):
                    Et = E[:, 512 * t:512 * (t + 1)].rearrange("p (c s) -> p c s", c=2)
                    last = V.scalar_tensor_tensor(Et, dist[:, t * S:(t + 1) * S].unsqueeze(1).to_broadcast([P, 2, S]),
                                                  -slope / HD ** -0.5, PS[:, b:b + 2, t * S:(t + 1) * S], ALU.mult, ALU.add)
                last.then_inc(unit_read, 1)
                dve.wait_ge(unit_read, u + 1)
                then(V.tensor_reduce(s[:, 0:4], E.rearrange("p (c s) -> p c s", c=4), AX_X, ALU.max))
                V.tensor_scalar(s[:, 0:4], s[:, 0:4], -HD ** -0.5, None, ALU.mult).then_inc(unit_arg, 1)

            def diff_combine(u):
                E, s = expo[:, u % 2, :], unit_s[:, u, :]
                dve.wait_ge(unit_exp, u + 1)
                then(V.reciprocal(s[:, 8:12], s[:, 4:8]))
                for t in range(NT):
                    last = V.tensor_scalar(s[:, 12 + t:13 + t], s[:, 9 + 2 * t:10 + 2 * t], lam[:, 5:6], None, ALU.mult)
                then(last)
                dve.wait_ge(unit_turned, u)
                for t in range(NT):
                    then(V.tensor_scalar(comb[:, t, :], E[:, 512 * t:512 * t + S], s[:, 8 + 2 * t:9 + 2 * t], None,
                                         ALU.mult))
                    last = V.scalar_tensor_tensor(comb[:, t, :], E[:, 512 * t + S:512 * (t + 1)], s[:, 12 + t:13 + t],
                                                  comb[:, t, :], ALU.mult, ALU.add)
                last.then_inc(unit_comb, 1)

            def unit_args(u):
                dve.wait_ge(unit_scored, u + 1)
                if u >= 2:
                    dve.wait_ge(unit_comb, u - 1)
                (mlstm_args if u < MH else diff_args)(u)

            dve.wait_ge(lam_set, 1)
            unit_args(0)
            for u in range(2 * MH + 1):
                if u + 1 < 2 * MH and u != MH - 1:
                    unit_args(u + 1)
                if u < MH:
                    mlstm_combine(u)
                elif u < 2 * MH:
                    diff_combine(u)
                if u == MH - 1:
                    unit_args(u + 1)
                if u >= 1:
                    dve.wait_ge(unit_out, u)
                    V.tensor_copy(work[:, :, (u - 1) * P:u * P], PS[:, 5, 0:S].rearrange("p (t n) -> p t n", t=NT))\
                        .then_inc(raw_set, 1)
            dve.wait_ge(raw_set, 8)

            for t in range(NT):
                for u in range(8):
                    last = V.bn_stats(bn6[:, 8 * t + u, :], work[:, t, u * P:(u + 1) * P])
            then(last)
            for n in range(16):
                last = V.bn_aggr(mv[:, n, :], bn6[:, n, :])
            then(last)
            var = bn6[:, :, 0]
            mvt = mv.rearrange("p (t u) c -> p t u c", t=NT)
            b6t = bn6.rearrange("p (t u) c -> p t u c", t=NT)
            then(V.tensor_tensor(b6t[:, :, 4:8, 1], mvt[:, :, 4:8, 0], mvt[:, :, 4:8, 0], ALU.mult))
            then(V.tensor_tensor(mvt[:, :, 4:8, 1], mvt[:, :, 4:8, 1], b6t[:, :, 4:8, 1], ALU.add))
            V.tensor_scalar(var, mv[:, :, 1], EPS, None, ALU.add).then_inc(var2_set, 1)
            dve.wait_ge(root2_set, 1)
            then(V.reciprocal(bn6[:, :, 3], bn6[:, :, 2]))
            dve.wait_ge(osig_set, 1)
            for t in range(NT):
                for u in range(8):
                    n = 8 * t + u
                    w = work[:, t, u * P:(u + 1) * P]
                    if u < MH:
                        last = V.tensor_scalar(w, w, mv[:, n, 0:1], bn6[:, n, 3:4], ALU.subtract, ALU.mult)
                    else:
                        last = V.tensor_scalar(w, w, bn6[:, n, 3:4], 1.0 - LAM_INIT, ALU.mult, ALU.mult)
                then(last)
                V.tensor_tensor(work[:, t, 0:MW], work[:, t, 0:MW], vo[:, t, MW:2 * MW], ALU.mult).then_inc(normed, 1)
            mixT = mixin[:, :, :].rearrange("p t d -> p (t d)").rearrange("p (k s) -> p k s", k=KD)
            place(TBRANCH, 0, mixT,
                  lambda k: colB[:, B_MLN + k:B_MLN + k + 1] if k < MH else colB[:, B_DNG:B_DNG + 1], None)
            residue_act(TBRANCH, mixT)
            residue_slot(dve, V, G_UP)
            residue_slot(dve, V, G_UP + 1)
            hflat = hT[:, :, :].rearrange("p k s -> p (k s)")
            for half in range(2):
                for br in range(2):
                    if half == 0:
                        residue_slot(dve, V, G_UP + 2 + br)
                    elif br == 0:
                        residue_slot(dve, V, G_WOUT2)
                    dve.wait_ge(slots_used, used(G_UP + 2 * half + br))
                    dve.wait_ge(gsig_set, 2 * half + br + 1)
                    ps = PS[:, 4 * half + 2 * br:4 * half + 2 * br + 2, :].rearrange("p b n -> p (b n)")
                    gate = gT[:, 8 * br + 4 * half:8 * br + 4 * half + 4, :].rearrange("p k s -> p (k s)")
                    dst = (hflat[:, 1024 * half:1024 * (half + 1)], work[:, half, :])[br]
                    last = V.tensor_tensor(dst, ps, gate, ALU.mult)
                then(last)
                V.tensor_tensor(hflat[:, 1024 * half:1024 * (half + 1)], hflat[:, 1024 * half:1024 * (half + 1)],
                                work[:, half, :], ALU.add).then_inc(mixed, 1)
            for half in range(2):
                ks = slice(4 * half, 4 * half + 4)
                dve.wait_ge(act_rounded, 2 * TMIXED + half + 1)
                V.tensor_tensor(hR[:, 1, ks, :], hT[:, ks, :], hR[:, 0, ks, :], ALU.subtract).then_inc(act_split, 1)
            residue_slot(dve, V, G_WOUT2 + 1)
            for i in range(N_WOUT2):
                if i < 2:
                    residue_slot(dve, V, G_WOUT2 + i + 2)
                dve.wait_ge(slots_used, used(G_WOUT2 + i))
                xs = xres[:, :, 256 * i:256 * (i + 1)]
                V.tensor_tensor(xs, xs, PS[:, i, :].rearrange("p (t n) -> p t n", t=NT), ALU.add).then_inc(x3_set, 1)
            dve.wait_ge(x3_set, 4)

            norm(N4)
            place(T4, 4, hT, lambda k: colB[:, B_NFFN + k:B_NFFN + k + 1], None)
            dve.wait_ge(logit16, 1)
            V.tensor_reduce(aff_s[:, 0:2], PS[:, 0, 0:32].rearrange("p (t e) -> p t e", t=NT), AX_X, ALU.max, negate=True)\
                .then_inc(negmax16, 1)
            dve.wait_ge(exp16, 1)
            then(V.reciprocal(aff_s[:, 4:6], aff_s[:, 2:4]))
            for t in range(NT):
                last = V.tensor_scalar(aff[:, t, :], aff[:, t, :], aff_s[:, 4 + t:5 + t], None, ALU.mult)
            last.then_inc(aff_set, 1)
            dve.wait_ge(aff_set, 1)

            def compare(q):
                dve.wait_ge(affbc_set, q + 1)
                if q >= 2:
                    dve.wait_ge(rank_cols, 2 * (q - 1))
                E = slice(4 * (q % 2), 4 * (q % 2) + 4)
                other = affbc[:, 4 * q:4 * q + 4, :]
                own = lambda i, n: aff[:, i, 4 * q:4 * q + 4].unsqueeze(2).to_broadcast([P, 4, n])
                V.tensor_tensor(beats[:, 0, E, 0:P], other[:, :, 0:P], own(0, P), ALU.is_lt)
                V.tensor_tensor(beats[:, 0, E, P:S], other[:, :, P:S], own(0, P), ALU.is_le)
                V.tensor_tensor(beats[:, 1, E, :], other, own(1, S), ALU.is_lt)
                for i in range(NT):
                    last = V.tensor_tensor(beats_eq[:, i, E, :], other[:, :, i * P:(i + 1) * P], own(i, P), ALU.is_equal)
                then(last)
                for i in range(NT):
                    last = V.tensor_tensor(beats_eq[:, i, E, :], beats_eq[:, i, E, :],
                                           tie.unsqueeze(1).to_broadcast([P, 4, P]), ALU.mult)
                last.then_inc(beats_set, 1)

            def choose(q):
                dve.wait_ge(rank_spread, q + 1)
                V.scalar_tensor_tensor(selTg[:, 2 * q:2 * q + 2, :].rearrange("p e t -> p (e t)"), PS[:, 4 + q % 2, :],
                                       slotcol, affbc[:, 2 * q:2 * q + 2, :].rearrange("p e t -> p (e t)"), ALU.is_equal,
                                       ALU.mult).then_inc(selT_set, 1)

            compare(0)
            for q in range(4):
                if q + 1 < 4:
                    compare(q + 1)
                choose(2 * q)
                choose(2 * q + 1)
            dve.wait_ge(rank_cols, 8)
            V.tensor_copy(rankc[:, :, :], PS[:, 6, 0:32].rearrange("p (t e) -> p t e", t=NT)).then_inc(rankc_set, 1)
            dve.wait_ge(rankc_set, 1)
            for t in range(NT):
                V.tensor_tensor(sel[:, t, :].rearrange("p (e c) -> p e c", e=EXPERTS),
                                slotrow.unsqueeze(1).to_broadcast([P, EXPERTS, CAP]),
                                rankc[:, t, :].unsqueeze(2).to_broadcast([P, EXPERTS, CAP]), ALU.is_equal)\
                    .then_inc(sel_set, 1)
            for k in range(KD):
                dve.wait_ge(gathered, k + 1)
                V.tensor_scalar(xeT[:, k, :], PS[:, k % 4, :], colB[:, B_NFFN + k:B_NFFN + k + 1], None, ALU.mult)\
                    .then_inc(xe_out, 1)

            with dve.Fori(0, EXPERTS) as e:
                dve.wait_ge(slots_used, e * PER_EXPERT + used(G_EXPERTS + 15))
                dve.wait_ge(silu_set, e + 1)
                V.tensor_tensor(hid[:, :], silu[:, :], PS[:, 1, :], ALU.mult).then_inc(hid_set, 1)
                dve.wait_ge(hid_turned, e + 1)
                V.tensor_copy(hidT[:, :, :, :].rearrange("p c j t -> p (c j t)"), PS[:, 2, :]).then_inc(hidT_set, 1)

            dve.wait_ge(scattered, EXPERTS + 1)
            for t in range(NT):
                V.tensor_copy(xres[:, t, :], PS[:, 4 + 2 * t:6 + 2 * t, :].rearrange("p b n -> p (b n)"))\
                    .then_inc(final_copied, 1)
            dve.wait_ge(gfinal_in, 16)
            for t in range(NT):
                V.scalar_tensor_tensor(work[:, t, :], xres[:, t, :], factor(NLAST, t), gfinal, ALU.mult, ALU.mult)\
                    .then_inc(final_set, 1)

        @block.scalar
        def _(act):
            N = nc.scalar
            then = Chain(act, act_chain)
            a0 = lambda ap: ap[0]

            act.dma_start(const[:, 0:P], A["shape_constants"][:, 0:P]).then_inc(ident_in, 16)
            act.dma_start(rowsA[A_GAIN:A_GAIN + 32, :], A["norm_gains"][0].rearrange("g (c p) -> (g c) p", p=P))\
                .then_inc(rows_in, 16)
            for at, n, name in ((A_BADA, 48, "b_ada"), (A_B1, 32, "b1")):
                act.dma_start(rowsA[at:at + n, :], A[name][0].rearrange("(c p) -> c p", p=P)).then_inc(rows_in, 16)
            act.dma_start(rowsB[B_CONVW:B_CONVW + 40, :], A["conv_w_2"][0].rearrange("j (c p) -> (j c) p", p=P))\
                .then_inc(rows_in, 16)
            for at, n, name in ((B_CONVB, 8, "conv_b_2"), (B_NMIX, 8, "norm_mix_g_2"), (B_NFFN, 8, "norm_ffn_g_2"),
                                (B_MLN, 4, "mlstm_norm_g_2"), (B_DNG, 1, "diff_norm_g_2"), (B_C, 8, "c")):
                act.dma_start(rowsB[at:at + n, :], A[name][0].rearrange("(c p) -> c p", p=P)).then_inc(rows_in, 16)
            act.dma_start(xres[:, :, :], A["x"][0].rearrange("(t p) d -> p t d", p=P)).then_inc(x_in, 16)

            def everywhere(row, n):
                return bass.AP(row.tensor, row.offset, [[0, P], [1, n]])

            act.dma_start(relb[:, :], A["rel_bias"]).then_inc(consts_in, 16)
            act.dma_start(const[:, P:C_END], A["shape_constants"][:, P:C_END]).then_inc(consts_in, 16)
            act.dma_start(sinkbc[:, :], everywhere(A["sinks"], 8)).then_inc(late_in, 16)
            act.dma_start(lambc[:, :, :].rearrange("p a d -> p (a d)"), everywhere(A["diff_lam_2"], 256)).then_inc(late_in, 16)
            act.dma_start(router[:, :, :], A["w_router_2"][0].rearrange("(k p) e -> p k e", p=P)).then_inc(late_in, 16)
            act.dma_start(mgate[:, :, :], w_in2[:, :, GATE0:GATE0 + 16]).then_inc(mg_in, 16)
            act.wait_ge(bmg_set, 1)
            for part, col, at in ((0, 0, 0), (0, 1, 4), (32, 0, 8), (32, 1, 12)):
                act.dma_start(bmg[part:part + 4, col:col + 1], A["b_mgate_2"][0, at:at + 4].rearrange("(a b) -> a b", b=1))\
                    .then_inc(mg_in, 16)
            act.dma_start(b2bc, everywhere(A["b2"], D)).then_inc(late_in, 16)
            act.dma_start(G1, everywhere(A["norm_gains"][0, 1], D)).then_inc(late_in, 16)
            act.dma_start(G2, everywhere(A["norm_gains"][0, 3], D)).then_inc(late_in, 16)

            def root(n, t, src, junk):
                N.activation(junk[:, t, :], src[:, t, :], ACT.Square, accum_out=stats[:, n, t:t + 1]).then_inc(squared, 1)
                act.wait_ge(squared, 2 * n + t + 1)
                N.activation(stats[:, n, 2 + t:3 + t], stats[:, n, t:t + 1], ACT.Sqrt, scale=1.0 / D, bias=eps[:, :])\
                    .then_inc(root_set, 1)

            def roots(n, src, junk, ready=None):
                for t in range(NT):
                    if ready:
                        act.wait_ge(ready, t + 1)
                    root(n, t, src, junk)

            def place(n, base, dst, scale, shift):
                for j in (1, 3):
                    act.wait_ge(turned, 4 * n + j + 1)
                    for q in range(4):
                        k = 4 * (j % 2) + q
                        o, i = dst[:, k, (j // 2) * P:(j // 2 + 1) * P], PS[:, base + j, q * P:(q + 1) * P]
                        last = N.activation(o, i, ACT.Identity, scale=scale(k), bias=(0.0 if shift is None else shift(k)))
                    last.then_inc(placed[1], 1)

            def round_act(n, src):
                for t in range(NT):
                    tile = slice(t * P, (t + 1) * P)
                    act.wait_ge(placed[0], 2 * n + t + 1)
                    act.wait_ge(placed[1], 2 * n + t + 1)
                    N.activation(hR[:, 0, :, tile], src[:, :, tile], ACT.Copy).then_inc(act_rounded, 1)

            act.wait_ge(cols_set, 1)
            N.activation(cact[:, :], colB[:, B_C:B_C + KD], ACT.Silu).then_inc(c_acted, 1)
            act.wait_ge(x_in, 16)
            act.wait_ge(ones_set, 3)
            roots(N1, xres, work)
            for g in range(G_WIN, G_WIN + 2):
                round_slot(act, g)
            act.wait_ge(folded, 1)
            shift1 = modcol[:, 0, 0:2, :].rearrange("p j q -> p (j q)")
            place(T1, 4, hT, lambda k: fold[:, 0, k:k + 1], lambda k: shift1[:, k:k + 1])
            round_act(T1, hT)
            for i in range(N_WIN):
                if i + 2 < N_WIN:
                    round_slot(act, G_WIN + i + 2)
                if i % 2 == 0:
                    continue
                act.wait_ge(slots_used, used(G_WIN + i))
                if i == 5:
                    N.activation(v1[:, :, 256:512], PS[:, i % 4, :].rearrange("p (t n) -> p t n", t=NT), ACT.Copy)\
                        .then_inc(win_out[1], 1)
                else:
                    chunk = {1: 2, 3: 6, 7: 10}[i]
                    N.activation(qk_chunks(chunk), PS[:, i % 4, :].rearrange("p (m s) -> p m s", m=4), ACT.Copy)\
                        .then_inc(win_out[1], 1)
            act.wait_ge(win_out[0], 5)
            for a, b in ((0, 64), (64, 0)):
                act.dma_start(qkT[a:a + 64, 13, :], qkT[b:b + 64, 12, :]).then_inc(kswap_in, 16)
            bg = A["b_ada"][0]
            act.dma_start(ybuf[:, 0, :], everywhere(bg[2 * D:3 * D], D)).then_inc(bg_in, 16)
            act.dma_start(ybuf[:, 1, :], everywhere(bg[5 * D:6 * D], D)).then_inc(bg_in, 16)

            act.wait_ge(lam_dots, 1)
            N.activation(lam[:, 2:4], lam[:, 0:2], ACT.Exp).then_inc(lam_exps, 1)
            for h in range(HEADS + 2):
                if h < HEADS:
                    s, L, Pr = att_s[:, h, :], logits[:, h % 2, :], probs[:, h % 2, :]
                    act.wait_ge(negmax_set, h + 1)
                    if h >= 2:
                        act.wait_ge(probs_turned, h - 1)
                    N.activation(Pr[:, 0:S], L[:, 0:S], ACT.Exp, bias=s[:, 0:1], accum_out=s[:, 2:3])
                    last = N.activation(Pr[:, S:384], L[:, S:384], ACT.Exp, bias=s[:, 1:2], accum_out=s[:, 3:4])
                    if h >= 8:
                        last = N.activation(s[:, 4:6], s[:, 0:2], ACT.Exp, bias=sinkbc[:, h - 8:h - 7])
                    last.then_inc(exp_set, 1)
                if 1 <= h <= HEADS:
                    g = h - 1
                    act.wait_ge(probs_turned, g + 1)
                    if g >= 2:
                        act.wait_ge(weighed, g - 1)
                    N.activation(probsT[:, g % 2, :].rearrange("p (b s) -> p b s", b=3)[:, :, ::-1],
                                 PS[:, 2 + g % 2, 0:384].rearrange("p (b s) -> p b s", b=3), ACT.Copy)\
                        .then_inc(probsT_set, 1)
                if h >= 2 and h % 2 == 1:
                    pair = (h - 2) // 2
                    act.wait_ge(weighed, 2 * pair + 2)
                    N.activation(hR[:, 0, pair, :], PS[:, 4 + pair % 2, 0:S], ACT.Copy).then_inc(att_rounded, 1)
            for g in range(G_WOUT, G_WOUT + 2):
                round_slot(act, g)
            for i in range(N_WOUT):
                if i < 3:
                    round_slot(act, after(G_WOUT + i))
                if i % 2 == 0:
                    continue
                act.wait_ge(slots_used, used(G_WOUT + i))
                N.activation(ybuf[:, :, 256 * i:256 * (i + 1)], PS[:, i, :].rearrange("p (t n) -> p t n", t=NT), ACT.Copy)\
                    .then_inc(wout_out[1], 1)
            act.wait_ge(wout_out[0], 2)
            act.wait_ge(wout_out[1], 2)
            roots(POST1, ybuf, work)
            roots(N2, xres, ybuf, x1_set)
            shift2 = modcol[:, 1, 2:4, :].rearrange("p j q -> p (j q)")
            place(T2, 4, hT, lambda k: fold[:, 1, k:k + 1], lambda k: shift2[:, k:k + 1])
            round_act(T2, hT)
            round_slot(act, G_MLP + 1)
            for half in range(2):
                for i in range(half * MLP_HALF, (half + 1) * MLP_HALF):
                    round_slot(act, after(g_w1(i)))
                    act.wait_ge(w1_relu, 2 * i + 2)
                    if i >= 2:
                        act.wait_ge(ff_split, i - 1)
                    c = 2 * (i % MLP_HALF)
                    N.activation(square[:, i % 2, :], relu[:, i % 2, :], ACT.Square)
                    N.activation(fR[:, 0, c:c + 2, :].rearrange("p m s -> p (m s)"), relu[:, i % 2, :], ACT.Square)\
                        .then_inc(w1_out, 1)
                for i in range(half * MLP_HALF, (half + 1) * MLP_HALF):
                    if g_w2(i) < G_MIX2 - 1:
                        round_slot(act, after(g_w2(i)))
            roots(POST2, ybuf, work, w2_out)
            roots(N3, xres, ybuf, x2_set)
            place(T3, 0, hT, lambda k: colB[:, B_NMIX + k:B_NMIX + k + 1], None)
            round_act(T3, hT)
            round_slot(act, G_MIX2 + 1)

            for i in range(N_MIX2):
                round_slot(act, G_MIX2 + i + 2)
                if i in range(4, 4 + 8):
                    c = i - 4
                    act.wait_ge(conv_set, c + 1)
                    N.activation(qkc[:, c, :], conv[:, c % 2, :], ACT.Silu).then_inc(qk_set, 1)
                if i % 2 == 0:
                    continue
                act.wait_ge(slots_used, used(G_MIX2 + i))
                turned_ = PS[:, i % 4, :].rearrange("p (m s) -> p m s", m=2)
                tokens_ = PS[:, i % 4, :].rearrange("p (t n) -> p t n", t=NT)
                if i == 1:
                    act.wait_ge(pads_set, 2)
                if i < 4:
                    dst, src = zpad[:, 2 * i:2 * i + 2, 2:2 + S], turned_
                elif i == 5:
                    dst, src = vo[:, :, 256:512], tokens_
                elif i < 10:
                    dst, src = dqk[:, 2 * (i - 6):2 * (i - 6) + 2, :], turned_
                elif i == 11:
                    dst, src = dv[:, :, 256:512], tokens_
                else:
                    dst, src = vo[:, :, MW + 256:2 * MW], tokens_
                N.activation(dst, src, ACT.Copy).then_inc(mix_out[1], 1)
                if i == 3:
                    R = rows2[0:36, :, :]
                    act.wait_ge(gate_rows_set, 1)
                    then(N.activation(R[:, 2, :], R[:, 2, :], ACT.Exp))
                    N.activation(R[:, 2, :], R[:, 2, :], ACT.Ln, bias=1.0).then_inc(gate_ln, 1)
                    act.wait_ge(gate_m, 2)
                    N.activation(R[:, 7, :], R[:, 7, :], ACT.Exp, scale=-1.0).then_inc(gate_em, 1)

            def unit_exps(u):
                E, s = expo[:, u % 2, :], unit_s[:, u, :]
                act.wait_ge(unit_arg, u + 1)
                if u < MH:
                    N.activation(E[:, 0:768], E[:, 0:768], ACT.Exp).then_inc(unit_exp, 1)
                else:
                    for n in range(4):
                        last = N.activation(E[:, n * S:(n + 1) * S], E[:, n * S:(n + 1) * S], ACT.Exp,
                                            scale=HD ** -0.5, bias=s[:, n:n + 1], accum_out=s[:, 4 + n:5 + n])
                    last.then_inc(unit_exp, 1)

            unit_exps(0)
            for u in range(2 * MH + 1):
                if u >= 1:
                    act.wait_ge(unit_turned, u)
                    if u >= 2:
                        act.wait_ge(unit_out, u - 1)
                    N.activation(combT[:, :, :].rearrange("p j s -> p (j s)"), PS[:, 4, :], ACT.Copy).then_inc(unit_T, 1)
                if u + 1 < 2 * MH:
                    unit_exps(u + 1)
                if u < 2 * MH:
                    round_slot(act, G_GATES2 + u + 2)
                    act.wait_ge(slots_used, used(G_GATES2 + u))
                    N.activation(gT[:, 2 * u:2 * u + 2, :].rearrange("p m s -> p (m s)"), PS[:, 6 + u % 2, :], ACT.Copy)\
                        .then_inc(gates_out, 1)
            act.wait_ge(mix_out[0], N_MIX2 // 2)
            N.activation(vo[:, :, MW:2 * MW], vo[:, :, MW:2 * MW], ACT.Sigmoid).then_inc(osig_set, 1)
            act.wait_ge(var2_set, 1)
            N.activation(bn6[:, :, 2], bn6[:, :, 0], ACT.Sqrt).then_inc(root2_set, 1)
            mixT = mixin[:, :, :].rearrange("p t d -> p (t d)").rearrange("p (k s) -> p k s", k=KD)
            place(TBRANCH, 0, mixT,
                  lambda k: colB[:, B_MLN + k:B_MLN + k + 1] if k < MH else colB[:, B_DNG:B_DNG + 1], None)
            round_act(TBRANCH, mixT)
            act.wait_ge(gates_out, 8)
            for half in range(2):
                for br in range(2):
                    if half == 0:
                        round_slot(act, G_UP + 2 + br)
                    elif br == 0:
                        round_slot(act, G_WOUT2)
                    g = gT[:, 8 * br + 4 * half:8 * br + 4 * half + 4, :].rearrange("p k s -> p (k s)")
                    N.activation(g, g, ACT.Sigmoid).then_inc(gsig_set, 1)
            act.wait_ge(slots_used, used(G_UP + N_UP - 1))
            for half in range(2):
                ks = slice(4 * half, 4 * half + 4)
                act.wait_ge(mixed, half + 1)
                N.activation(hR[:, 0, ks, :], hT[:, ks, :], ACT.Copy).then_inc(act_rounded, 1)
            for g in range(G_WOUT2 + 1, G_WOUT2 + N_WOUT2):
                round_slot(act, g)
            act.wait_ge(x3_set, 4)
            roots(N4, xres, ybuf)
            place(T4, 4, hT, lambda k: colB[:, B_NFFN + k:B_NFFN + k + 1], None)
            act.wait_ge(negmax16, 1)
            for t in range(NT):
                last = N.activation(aff[:, t, :], PS[:, 0, t * EXPERTS:(t + 1) * EXPERTS], ACT.Exp,
                                    bias=aff_s[:, t:t + 1], accum_out=aff_s[:, 2 + t:3 + t])
            last.then_inc(exp16, 1)
            for q in range(4):
                act.wait_ge(aff_spread, q + 1)
                b = 2 * (q % 2)
                N.activation(affbc[:, 4 * q:4 * q + 4, :].rearrange("p e t -> p (e t)"),
                             PS[:, b:b + 2, :].rearrange("p b n -> p (b n)"), ACT.Copy).then_inc(affbc_set, 1)
            act.dma_start(gfinal, everywhere(A["norm_f_g_2"], D)).then_inc(gfinal_in, 16)
            act.wait_ge(selT_set, 8)
            with act.Fori(0, EXPERTS) as e:
                act.wait_ge(slots_used, e * PER_EXPERT + used(G_EXPERTS + 7))
                N.activation(silu[:, :], PS[:, 0, :], ACT.Silu).then_inc(silu_set, 1)
                act.wait_ge(slots_used, e * PER_EXPERT + used(G_EXPERTS + 23))
                N.activation(ye[:, :], PS[:, 3, :], ACT.Copy).then_inc(ye_set, 1)
            roots(NLAST, xres, work, final_copied)

        @block.gpsimd
        def _(pool):
            G = nc.gpsimd
            then = Chain(pool, pool_chain)
            pool.wait_ge(bias_row_set, 1)
            pool.dma_start(bias_scratch, logits[0:HEADS, 0, :]).then_inc(bias_stored, 16)
            pool.wait_ge(bias_stored, 16)
            for h in range(HEADS):
                src = bass.AP(bias_scratch.tensor, bias_scratch.offset + h * 384, [[1, P], [1, S]])
                pool.dma_start(biasm[:, h, 0:S], src).then_inc(bias_in, 16)
            pool.wait_ge(bias_in, 16 * HEADS)
            G.tensor_copy(biasm[:, :, S:384], biasm[:, :, P:S]).then_inc(bias_copied, 1)
            residue_slot(pool, G, BY_POOL[0])
            pool.wait_ge(x2_set, 2)
            G.memset(zpad[:, :, 0:2], 0.0)
            G.memset(zpad[:, :, S + 2:S + 4], 0.0).then_inc(pads_set, 1)
            G.memset(rows2[0:36, :, :], 0.0).then_inc(pads_set, 1)
            pool.wait_ge(mg_in, 16 * 5)
            pool.wait_ge(root_set, 2 * N3 + 2)
            G.memset(wgi, 0.0)
            then(G.memset(wgf, 0.0))
            for w, at in ((wgi, 0), (wgf, 4)):
                for d in range(2):
                    G.tensor_copy(w[:, :, 32 * d:32 * d + 4], mgate[:, :, at + 8 * d:at + 8 * d + 4]).then_inc(wg_set, 1)
            for g in BY_POOL[1:]:
                residue_slot(pool, G, g)
            pool.wait_ge(xe_out, KD)
            pool.wait_ge(selT_set, 8)
            with pool.Fori(0, EXPERTS) as e:
                pool.wait_ge(slots_used, e * PER_EXPERT + used(G_EXPERTS + 15 - PER_EXPERT))
                G.tensor_copy(xe[:, :, :], xeT[:, :, bass.ds(e * CAP, CAP)]).then_inc(xe_ready, 1)
                pool.wait_ge(scattered, e + 1)
                G.tensor_copy(selx[:, :], selTg[:, bass.ds(e, 1), :].rearrange("p o t -> p (o t)"))\
                    .then_inc(selx_ready, 1)


_INS = ["x", "c", "w_in", "w_out", "sinks", "rel_bias", "w_ada", "b_ada", "norm_gains", "w1", "b1", "w2", "b2",
        "norm_mix_g_2", "w_in_2", "b_mgate_2", "conv_w_2", "conv_b_2", "mlstm_norm_g_2", "diff_lam_2", "diff_norm_g_2",
        "w_up_a_2", "w_up_b_2", "w_out_2", "norm_ffn_g_2", "w_router_2", "w_gate_e_2", "w_up_e_2", "w_down_e_2",
        "norm_f_g_2"]


def kernel(**inputs):
    import concourse.bacc as _bacc
    from concourse.bass_utils import run_bass_kernel_spmd as _run

    nc = _bacc.Bacc("TRN2", target_bir_lowering=False, num_devices=1)
    arrays, aps = {}, {}
    for name in _INS + ["shape_constants"]:
        a = shape_constants() if name == "shape_constants" else np.ascontiguousarray(inputs[name])
        if name == "norm_f_g_2":
            a = a.reshape(1, D)
        arrays[f"in_{name}"] = a
        aps[name] = nc.dram_tensor(f"in_{name}", a.shape, mybir.dt.from_np(a.dtype), kind="ExternalInput").ap()
    out = nc.dram_tensor("out", (1, S, D), F32, kind="ExternalOutput").ap()
    bias_scratch = nc.dram_tensor("bias_scratch", [HEADS, 384], F32, kind="Internal").ap()
    build_program(nc, aps, out, bias_scratch)
    r = _run(nc, [arrays], core_ids=[0])
    return r.results[0]["out"]
```
